# Optimizing a Trainium2 kernel written in Bass

```python
import math
import jax, jax.numpy as jnp
from jax import lax
import numpy as np

D_MODEL = 1024
BATCH = 1
SEQ = 512
DEPTH = 1

CHUNK = 64
N_MEM = 256
EPS = 1e-6
A_HEADS = 16
A_KV_HEADS = 2
A_HEAD_DIM = 64
A_GROUP = A_HEADS // A_KV_HEADS
WINDOW = 128
WIN_CHUNKS = WINDOW // CHUNK
KEY_SPAN = WIN_CHUNKS * CHUNK
REL_BUCKETS = 32
REL_MAX_DIST = WINDOW
X_HEADS = 4
X_HEAD_DIM = 128
POOL_WINDOWS = (2, 4, 8, 16)
POOL_GROUPS = len(POOL_WINDOWS)
POOL_GROUP_DIM = 128
POOL_WIDTH = POOL_GROUPS * POOL_GROUP_DIM
N_BRANCH = 3
D_FF = -(-8 * D_MODEL // 768) * 256

A_Q = A_HEADS * A_HEAD_DIM
A_KV = A_KV_HEADS * A_HEAD_DIM
X_Q = X_HEADS * X_HEAD_DIM
IN_COLS = A_Q + 2 * A_KV + X_Q + POOL_WIDTH + N_BRANCH * D_MODEL

kernel_name = "hybrid_swa_sink_pool_memxattn_block"

def rms_norm(x, g):
    xf = x.astype(jnp.float32)
    y = xf * lax.rsqrt(jnp.mean(xf * xf, axis=-1, keepdims=True) + EPS)
    return (y * g.astype(jnp.float32)).astype(x.dtype)

def t5_bucket_ids():
    q = np.arange(CHUNK)[:, None]
    k = np.arange(-(WIN_CHUNKS - 1) * CHUNK, CHUNK)[None, :]
    rel = k - q
    nb = REL_BUCKETS // 2
    max_exact = nb // 2
    n = np.abs(rel)
    large = max_exact + (np.log(np.maximum(n, 1) / max_exact)
                         / np.log(REL_MAX_DIST / max_exact) * (nb - max_exact)).astype(np.int32)
    large = np.minimum(large, nb - 1)
    return ((rel > 0).astype(np.int32) * nb + np.where(n < max_exact, n, large)).astype(np.int32)

def window_attention(q, k, v, rel_bias, sinks):
    B, S = q.shape[0], q.shape[1]
    nc = S // CHUNK
    qb = q.reshape(B, nc, CHUNK, A_KV_HEADS, A_GROUP, A_HEAD_DIM)
    kc = k.reshape(B, nc, CHUNK, A_KV_HEADS, A_HEAD_DIM)
    vc = v.reshape(B, nc, CHUNK, A_KV_HEADS, A_HEAD_DIM)

    def band(t):
        parts = [jnp.pad(t, ((0, 0), (j, 0), (0, 0), (0, 0), (0, 0)))[:, :nc]
                 for j in range(WIN_CHUNKS - 1, -1, -1)]
        return jnp.concatenate(parts, axis=2)

    kb, vb = band(kc), band(vc)
    s = jnp.einsum('bcqgrd,bckgd->bcgrqk', qb, kb).astype(jnp.float32) * (A_HEAD_DIM ** -0.5)
    bias = rel_bias.astype(jnp.float32)[t5_bucket_ids()]
    bias = jnp.transpose(bias, (2, 0, 1)).reshape(A_KV_HEADS, A_GROUP, CHUNK, KEY_SPAN)
    s = s + bias
    key_chunk = (np.arange(nc)[:, None] - (WIN_CHUNKS - 1)
                 + np.arange(KEY_SPAN)[None, :] // CHUNK)
    valid = key_chunk >= 0
    s = jnp.where(valid[None, :, None, None, None, :], s, -1e30)
    sink = jnp.broadcast_to(sinks.astype(jnp.float32).reshape(A_KV_HEADS, A_GROUP, 1, 1),
                            s.shape[:-1] + (1,))
    p = jax.nn.softmax(jnp.concatenate([s, sink], axis=-1), axis=-1)[..., :-1]
    o = jnp.einsum('bcgrqk,bckgd->bcqgrd', p.astype(vb.dtype), vb)
    return o.reshape(B, S, A_Q)

def memory_attention(q, mk, mv):
    B, S = q.shape[0], q.shape[1]
    s = jnp.einsum('bshd,bmhd->bhsm', q, mk).astype(jnp.float32) * (X_HEAD_DIM ** -0.5)
    p = jax.nn.softmax(s, axis=-1)
    o = jnp.einsum('bhsm,bmhd->bshd', p.astype(mv.dtype), mv)
    return o.reshape(B, S, X_Q)

def multiscale_pool(p, w_map, scale):
    B, S = p.shape[0], p.shape[1]
    pg = p.reshape(B, S, POOL_GROUPS, POOL_GROUP_DIM)
    count = jnp.arange(1, S + 1, dtype=jnp.float32)[:, None]
    outs = []
    for g, w in enumerate(POOL_WINDOWS):
        xg = pg[:, :, g].astype(jnp.float32)
        cs = jnp.cumsum(xg, axis=1)
        lag = jnp.pad(cs, ((0, 0), (w, 0), (0, 0)))[:, :S]
        mean = (cs - lag) / jnp.minimum(count, float(w))
        outs.append(mean - xg)
    d = jnp.stack(outs, axis=2).astype(p.dtype)
    y = jnp.einsum('bsgc,gcd->bsgd', d, w_map).reshape(B, S, POOL_WIDTH)
    return y * scale

def setup_inputs(seed: int = 0) -> dict:
    key = jax.random.key(seed)
    ks = jax.random.split(key, 24)
    f32 = jnp.float32

    def nrm(k, shape, fan_in):
        return jax.random.normal(k, shape, f32) * (fan_in ** -0.5)

    def gain(k, shape):
        return jnp.ones(shape, f32) + 0.02 * jax.random.normal(k, shape, f32)

    L = DEPTH
    return {
        "x": jax.random.normal(ks[0], (BATCH, SEQ, D_MODEL), f32),
        "mem": jax.random.normal(ks[1], (BATCH, N_MEM, D_MODEL), f32),
        "norm_mix_pre": gain(ks[2], (L, D_MODEL)),
        "norm_mix_post": gain(ks[3], (L, D_MODEL)),
        "norm_mem": gain(ks[4], (L, D_MODEL)),
        "w_in": nrm(ks[5], (L, D_MODEL, IN_COLS), D_MODEL),
        "rel_bias": 0.1 * jax.random.normal(ks[6], (REL_BUCKETS, A_HEADS), f32),
        "attn_sinks": 0.5 * jax.random.normal(ks[7], (L, A_HEADS), f32),
        "w_mem_kv": nrm(ks[8], (L, D_MODEL, 2 * X_Q), D_MODEL),
        "w_pool_map": nrm(ks[9], (L, POOL_GROUPS, POOL_GROUP_DIM, POOL_GROUP_DIM), POOL_GROUP_DIM),
        "pool_scale": gain(ks[10], (L, POOL_WIDTH)),
        "w_branch_a": nrm(ks[11], (L, A_Q, D_MODEL), A_Q),
        "w_branch_x": nrm(ks[12], (L, X_Q, D_MODEL), X_Q),
        "w_branch_p": nrm(ks[13], (L, POOL_WIDTH, D_MODEL), POOL_WIDTH),
        "w_out": nrm(ks[14], (L, D_MODEL, D_MODEL), D_MODEL),
        "norm_ffn_pre": gain(ks[15], (L, D_MODEL)),
        "norm_ffn_post": gain(ks[16], (L, D_MODEL)),
        "w_ffn_gate": nrm(ks[17], (L, D_MODEL, D_FF), D_MODEL),
        "w_ffn_up": nrm(ks[18], (L, D_MODEL, D_FF), D_MODEL),
        "w_ffn_down": nrm(ks[19], (L, D_FF, D_MODEL), D_FF),
    }

def reference(x, mem, norm_mix_pre, norm_mix_post, norm_mem, w_in, rel_bias, attn_sinks,
              w_mem_kv, w_pool_map, pool_scale, w_branch_a, w_branch_x, w_branch_p, w_out,
              norm_ffn_pre, norm_ffn_post, w_ffn_gate, w_ffn_up, w_ffn_down):
    B, S = x.shape[0], x.shape[1]
    cut = np.cumsum([A_Q, A_KV, A_KV, X_Q, POOL_WIDTH]).tolist()
    for l in range(DEPTH):
        h = rms_norm(x, norm_mix_pre[l])
        z = h @ w_in[l]
        qa, ka, va, qx, pin, gl = jnp.split(z, cut, axis=-1)
        gates = jax.nn.sigmoid(gl.astype(jnp.float32)).astype(x.dtype).reshape(B, S, N_BRANCH, D_MODEL)

        oa = window_attention(qa.reshape(B, S, A_HEADS, A_HEAD_DIM),
                              ka.reshape(B, S, A_KV_HEADS, A_HEAD_DIM),
                              va.reshape(B, S, A_KV_HEADS, A_HEAD_DIM),
                              rel_bias, attn_sinks[l])
        ya = oa @ w_branch_a[l]

        mkv = rms_norm(mem, norm_mem[l]) @ w_mem_kv[l]
        mk, mv = jnp.split(mkv, 2, axis=-1)
        ox = memory_attention(qx.reshape(B, S, X_HEADS, X_HEAD_DIM),
                              mk.reshape(B, N_MEM, X_HEADS, X_HEAD_DIM),
                              mv.reshape(B, N_MEM, X_HEADS, X_HEAD_DIM))
        yx = ox @ w_branch_x[l]

        op = multiscale_pool(pin, w_pool_map[l], pool_scale[l])
        yp = op @ w_branch_p[l]

        merged = gates[:, :, 0] * ya + gates[:, :, 1] * yx + gates[:, :, 2] * yp
        x = x + rms_norm(merged @ w_out[l], norm_mix_post[l])

        h = rms_norm(x, norm_ffn_pre[l])
        f = (jax.nn.silu(h @ w_ffn_gate[l]) * (h @ w_ffn_up[l])) @ w_ffn_down[l]
        x = x + rms_norm(f, norm_ffn_post[l])
    return x


_drawn_inputs = setup_inputs


def setup_inputs(seed=0):
    import zlib

    import numpy as np

    out = dict(_drawn_inputs(seed))
    spreads = {}
    factors = {'norm_mix_pre': 3.073,
     'norm_mix_post': 3.653,
     'norm_mem': 8.0,
     'rel_bias': 14.997,
     'attn_sinks': 64.0,
     'pool_scale': 9.841,
     'norm_ffn_pre': 3.447,
     'norm_ffn_post': 51.976}
    for name, (base, spread) in spreads.items():
        noise = np.random.default_rng([zlib.crc32(name.encode()), seed]).standard_normal(out[name].shape)
        drawn = base * np.exp(spread * noise) if base else spread * noise
        out[name] = __import__('jax').numpy.asarray(drawn.astype(out[name].dtype))
    for name, factor in factors.items():
        out[name] = (out[name] * factor).astype(out[name].dtype)
    return out
```

```python
import math
from contextlib import ExitStack

import numpy as np

import concourse.bass as bass
from concourse import mybir

F32 = mybir.dt.float32
F32R = mybir.dt.float32r
BF16 = mybir.dt.bfloat16
ALU = mybir.AluOpType
ACT = mybir.ActivationFunctionType
AX_X = mybir.AxisListType.X

P = 128
SEQ, D, N_MEM = 512, 1024, 256
TT, MT, KT = SEQ // P, N_MEM // P, D // P
CHUNK = 64
NC_ = SEQ // CHUNK
A_HEADS, HD, GROUPS = 16, 64, 2
KEYS = 2 * CHUNK
X_HEADS = 4
POOL_WINDOWS = (2, 4, 8, 16)
PAD = 16
D_FF = 2816
FT = D_FF // P
EPS = 1e-6
A_SCALE = float(HD) ** -0.5
X_SCALE = float(P) ** -0.5
REL_BUCKETS = 32

K_COL = A_HEADS * HD
V_COL = K_COL + P
QX_COL = V_COL + P
PIN_COL = QX_COL + X_HEADS * P
GATE_COL = PIN_COL + 4 * P

A_UNITS = GROUPS * NC_
X_UNITS = X_HEADS * 2
UNITS = A_UNITS + X_UNITS

KB = 1024


def bucket_ranges():
    rel = np.arange(-(KEYS - 1), CHUNK)[::-1]
    nb, n = REL_BUCKETS // 2, np.abs(rel)
    exact = nb // 2
    large = exact + (np.log(np.maximum(n, 1) / exact) / np.log(KEYS / exact) * (nb - exact)).astype(np.int32)
    ids = (rel > 0) * nb + np.where(n < exact, n, np.minimum(large, nb - 1))
    cuts = [0] + [i for i in range(1, len(ids)) if ids[i] != ids[i - 1]] + [len(ids)]
    return [(a, b, int(ids[a])) for a, b in zip(cuts, cuts[1:])]


def plan():
    steps = [[("mem", h)] for h in range(2 * X_HEADS)]
    steps += [[("k", 0)], [("v", 0)]]
    steps += [[("q", j)] for j in range(8)]
    steps += [[("qx", h)] for h in range(X_HEADS)]
    steps += [[("pin", g)] for g in range(4)]

    def gates(jp):
        return [[("gate", 6 * jp + 2 * b + i)] for b in range(3) for i in range(2)]

    def merge(jp):
        a = [[("a", 2 * jp)], [("a", 2 * jp + 1)]]
        return a + [[("p", j), ("x", j)] for j in (2 * jp, 2 * jp + 1)]

    steps += gates(0) + gates(1)
    steps += merge(0) + gates(2) + merge(1) + gates(3) + merge(2) + merge(3)
    first = steps.index([("pin", 0)])
    for g in range(4):
        steps[first + 3 + 2 * g].append(("map", g))
    n = len(steps)
    stream = [("step", s) for s in range(n)]
    for c, at in ((1, n - 2), (0, n - 6)):
        stream[at:at] = [("out", 2 * c), ("out", 2 * c + 1)]
    stream += [("out", k) for k in range(4, KT)]
    stream += [("ffn", e) for e in range(2 * FT)]
    stream += [("down", k) for k in range(FT)]
    return steps, stream


def encoder_block(nc, x, mem, g_mix_pre, g_mix_post, g_mem, w_in, rel_bias, sinks, w_mem_kv, w_pool_map,
                  pool_scale, w_branch_a, w_branch_x, w_branch_p, w_out, g_ffn_pre, g_ffn_post,
                  w_gate, w_up, w_down, out):
    steps, stream = plan()
    NS = len(steps)
    tiles = [t for s in steps for t in s]
    tile_no = {t: n for n, t in enumerate(tiles)}
    step_end = np.cumsum([len(s) for s in steps]).tolist()
    at_stream = {g: n for n, g in enumerate(stream)}
    UNIT0 = steps.index([("q", 4)])

    copied_kinds = ("mem", "k", "v", "q", "qx", "pin", "gate")
    copied_no, merged_no = {}, {}
    for t in tiles:
        d = copied_no if t[0] in copied_kinds else merged_no
        d[t] = len(d) + 1

    def ap(t, offset, pattern):
        return bass.AP(t.tensor, t.offset + offset, pattern)

    def row_bcast(v, n=D):
        return ap(v, 0, [[0, P], [1, n]])

    BASE = 16512

    def sb(name, kb, shape, dt=F32):
        return nc.alloc_sbuf_tensor_at(name, shape, dt, offset=BASE + int(kb * KB))

    raw = [sb(f"raw{i}", 8 * i, [P, 2, 1024]) for i in range(2)]
    narrow_at = [16, 24, 32, 196]
    w_hi = [sb(f"w_hi{i}", a, [P, 8, P], F32R) for i, a in enumerate(narrow_at)]
    w_lo = [sb(f"w_lo{i}", a + 4, [P, 8, P], F32R) for i, a in enumerate(narrow_at)]
    hT_hi, hT_lo = sb("hT_hi", 40, [P, KT, SEQ], F32R), sb("hT_lo", 56, [P, KT, SEQ], F32R)
    memT_hi, memT_lo = sb("memT_hi", 72, [P, KT, N_MEM], F32R), sb("memT_lo", 80, [P, KT, N_MEM], F32R)
    gates = sb("gates", 72, [P, 12, SEQ])
    k_dup = sb("k_dup", 96, [P, GROUPS, CHUNK + SEQ])
    v_c = sb("v_c", 100.5, [P, NC_, P])
    bias = sb("bias", 104.5, [P, GROUPS, 4, KEYS])
    mv = sb("mv", 108.5, [P, MT, X_HEADS, P])
    probs = [sb(f"probs{i}", 112.5 + 2 * i, [P, 4, P]) for i in range(2)]
    probsT = sb("probsT", 116.5, [P, 4, P])
    pooled = [sb(f"pooled{i}", 118.5 + 2.0625 * i, [P, PAD + SEQ]) for i in range(4)]
    vT = sb("vT", 118.5, [P, CHUNK + SEQ])
    mrg_hi, mrg_lo = sb("mrg_hi", 96, [P, KT, SEQ], F32R), sb("mrg_lo", 112, [P, KT, SEQ], F32R)
    oa_hi, oa_lo = sb("oa_hi", 128, [P, 8, SEQ], F32R), sb("oa_lo", 144, [P, 8, SEQ], F32R)
    x_in = sb("x_in", 128, [P, TT, D])
    mem_in = sb("mem_in", 144, [P, MT, D])
    square0 = sb("square0", 152, [P, D])
    g_mem_b = sb("g_mem_b", 156, [P, D])
    q = sb("q", 160, [P, 4, NC_, 2, CHUNK])
    g_mix_pre_b = sb("g_mix_pre_b", 172, [P, D])
    ox_hi, ox_lo = sb("ox_hi", 160, [P, 4, SEQ], F32R), sb("ox_lo", 168, [P, 4, SEQ], F32R)
    op_hi, op_lo = sb("op_hi", 176, [P, 4, SEQ], F32R), sb("op_lo", 184, [P, 4, SEQ], F32R)
    mvT = sb("mvT", 176, [P, X_HEADS, N_MEM])
    rel_row = sb("rel_row", 180, [A_HEADS, 192])
    bias_back = sb("bias_back", 184, [P, GROUPS, 4, KEYS])
    relT = sb("relT", 181, [A_HEADS, REL_BUCKETS])
    qx = sb("qx", 192, [P, X_HEADS, SEQ])
    mk = sb("mk", 200, [P, X_HEADS, N_MEM])
    mixed = [sb(f"mixed{i}", 192 + 2 * i, [P, SEQ]) for i in range(2)]
    part = sb("part", 200, [P, SEQ])
    out_at = [40, 48, 56, 64, 72, 80, 88, 196]
    wo_hi = [sb(f"wo_hi{k}", a, [P, D], F32R) for k, a in enumerate(out_at)]
    wo_lo = [sb(f"wo_lo{k}", a + 4, [P, D], F32R) for k, a in enumerate(out_at)]
    x1 = sb("x1", 128, [P, TT, D])
    g_post_b = sb("g_post_b", 144, [P, D])
    h2T_hi, h2T_lo = sb("h2T_hi", 148, [P, KT, SEQ], F32R), sb("h2T_lo", 164, [P, KT, SEQ], F32R)
    y = [sb(f"y{i}", 180 + 4 * i, [P, D]) for i in range(2)]
    g_ffn_pre_b = sb("g_ffn_pre_b", 188, [P, D])
    f_hi, f_lo = sb("f_hi", 40, [P, FT, SEQ], F32R), sb("f_lo", 84, [P, FT, SEQ], F32R)
    silu = [sb(f"silu{i}", 180 + 2 * i, [P, SEQ]) for i in range(2)]
    prod = [sb(f"prod{i}", 184 + 2 * i, [P, SEQ]) for i in range(2)]
    down_at = [188, 16, 24, 32, 196, 148, 156, 164, 172]
    ND = len(down_at)
    wd_hi = [sb(f"wd_hi{k}", a, [P, D], F32R) for k, a in enumerate(down_at)]
    wd_lo = [sb(f"wd_lo{k}", a + 4, [P, D], F32R) for k, a in enumerate(down_at)]
    w_map = sb("w_map", 204, [P, 4, P])
    square1 = sb("square1", 204, [P, D], BF16)
    ident = sb("ident", 206, [P, P])
    small_at = [206.5]

    def small(name, shape):
        t = sb(name, small_at[0], shape)
        small_at[0] += 32 * math.ceil(4 * int(np.prod(shape[1:])) / 32) / KB
        return t

    sink = small("sink", [P, GROUPS, 4])
    scale_p = small("scale_p", [P, 4])
    inv_count = small("inv_count", [P, PAD])
    minus_half = small("minus_half", [P, 1])
    sumsq = small("sumsq", [P, 20])
    meansq = small("meansq", [P, 20])
    rstd = small("rstd", [P, 20])
    row_max = [small(f"row_max{i}", [P, 4]) for i in range(2)]
    neg_max = [small(f"neg_max{i}", [P, 4]) for i in range(2)]
    sink_gap = [small(f"sink_gap{i}", [P, 4]) for i in range(2)]
    row_sum = [small(f"row_sum{i}", [P, 4]) for i in range(2)]
    denom = [small(f"denom{i}", [P, 4]) for i in range(2)]
    inv_denom = [small(f"inv_denom{i}", [P, 4]) for i in range(2)]
    assert small_at[0] <= 207.8

    rel_dram = nc.dram_tensor("rel_scratch", [A_HEADS, 192], F32, kind="Internal").ap()

    NORM_MEM, NORM_X, NORM_MIX, NORM_POST = 0, MT, MT + TT, MT + 3 * TT

    with ExitStack() as ctx:
        pair = [ctx.enter_context(nc.psum_tensor(f"pair{i}", [P, 2, SEQ], F32)) for i in range(4)]

        def bk(i):
            return pair[i // 2][:, i % 2, :]

        def row_banks(t):
            return pair[t][:, :, :].rearrange("p a b -> p (a b)")

        scores = pair[2]

        def sem(name):
            return ctx.enter_context(nc.semaphore(name))

        raw_in = [sem(f"raw_in{i}") for i in range(2)]
        mem_loaded = [sem(f"mem_loaded{i}") for i in range(MT)]
        x_loaded = [sem(f"x_loaded{i}") for i in range(TT)]
        x_again = [sem(f"x_again{i}") for i in range(TT)]
        gain_loaded = {n: sem(f"gain_{n}") for n in ("mem", "pre", "post", "ffn_pre", "ffn_post")}
        rel_loaded, rel_built, rel_saved, bias_loaded = (sem(n) for n in ("rel_loaded", "rel_built", "rel_saved", "bias_loaded"))
        smalls_loaded = sem("smalls_loaded")
        consts_ready, pads_ready = sem("consts_ready"), sem("pads_ready")
        pool_chain, vec_chain = sem("pool_chain"), sem("vec_chain")
        weights_hi, weights_split = sem("weights_hi"), sem("weights_split")
        squares_summed, rstd_ready = sem("squares_summed"), sem("rstd_ready")
        rows_normed, rows_turned, turned_hi, turned_split = (sem(n) for n in ("rows_normed", "rows_turned", "turned_hi", "turned_split"))
        tile_full, tile_copied, tile_merged = sem("tile_full"), sem("tile_copied"), sem("tile_merged")
        scores_full, scores_read, neg_max_ready, exps_done = (sem(n) for n in ("scores_full", "scores_read", "neg_max_ready", "exps_done"))
        probs_ready, probs_turned, probsT_ready = (sem(n) for n in ("probs_ready", "probs_turned", "probsT_ready"))
        o_full, o_hi_done, o_split = sem("o_full"), sem("o_hi_done"), sem("o_split")
        pool_diff_ready, map_hi_done = sem("pool_diff_ready"), sem("map_hi_done")
        sigmoid_ready, mixed_ready, mrg_hi_done, mrg_split = (sem(n) for n in ("sigmoid_ready", "mixed_ready", "mrg_hi_done", "mrg_split"))
        out_full, x1_ready, h2_ready = sem("out_full"), sem("x1_ready"), sem("h2_ready")
        ffn_full, silu_ready, prod_ready, f_hi_done, f_split = (sem(n) for n in ("ffn_full", "silu_ready", "prod_ready", "f_hi_done", "f_split"))
        down_used, down_full, result_ready, stored = (sem(n) for n in ("down_used", "down_full", "result_ready", "stored"))

        w_in_v = w_in.rearrange("(k p) n -> p k n", p=P)
        w_mem_v = w_mem_kv.rearrange("(k p) n -> p k n", p=P)
        gate_v, up_v = (w.rearrange("(k p) n -> p k n", p=P) for w in (w_gate, w_up))
        wa_v = w_branch_a.rearrange("(k p) n -> p k n", p=P)
        wp_v, wx_v = (w.rearrange("(k p) n -> p k n", p=P) for w in (w_branch_p, w_branch_x))

        def chunk_halves(first):
            kind, n = first
            if kind in ("out", "down"):
                w = w_out if kind == "out" else w_down
                return [w[P * (n + i):P * (n + i + 1), :] for i in range(2)]
            if kind == "ffn":
                v, col = (gate_v, up_v)[(n // 2) % 2], 2 * P * (n // 4)
            else:
                t, i = steps[n][0]
                if t == "p":
                    return [v[:, :, P * i:P * i + 2 * P] for v in (wp_v, wx_v)]
                if t == "mem":
                    v, col = w_mem_v, P * i
                elif t == "a":
                    v, col = wa_v, P * i
                elif t == "gate":
                    v, col = w_in_v, GATE_COL + D * (i % 6 // 2) + 2 * P * (i // 6)
                else:
                    v, col = w_in_v, {"k": K_COL, "q": 0, "qx": QX_COL, "pin": PIN_COL}[t] + P * i
            return [v[:, 4 * h:4 * h + 4, col:col + 2 * P] for h in range(2)]

        def raw_view(s):
            r = raw[s // 2 % 2]
            if stream[s][0] in ("out", "down"):
                return r[:, s % 2, :]
            return r[:, :, :].rearrange("p a (k c) -> p (a k) c", c=2 * P)[:, :, P * (s % 2):P * (s % 2) + P]

        def split_at(s):
            kind, n = stream[s]
            if kind == "step":
                return w_hi[n % 3][:, :, :], w_lo[n % 3][:, :, :]
            if kind == "ffn":
                return w_hi[n % 4][:, :, :], w_lo[n % 4][:, :, :]
            if kind == "out":
                return wo_hi[n][:, :], wo_lo[n][:, :]
            return wd_hi[n % ND][:, :], wd_lo[n % ND][:, :]

        def wait_split_free(eng, s):
            kind, n = stream[s]
            if kind == "step" and n >= 3:
                eng.wait_ge(tile_full, step_end[n - 3])
            elif kind == "out" and n < 4:
                eng.wait_ge(tile_full, tile_no[("gate", 23)] + 1)
            elif kind == "out":
                eng.wait_ge(tile_full, len(tiles))
                eng.wait_ge(mrg_split, KT)
            elif kind == "ffn" and n < 3:
                eng.wait_ge(tile_full, len(tiles))
            elif kind == "ffn" and n == 3:
                eng.wait_ge(out_full, TT)
            elif kind == "ffn":
                eng.wait_ge(ffn_full, n - 3)
            elif kind == "down" and n == 0:
                eng.wait_ge(h2_ready, TT)
            elif kind == "down" and n < 4:
                eng.wait_ge(ffn_full, 2 * FT - 4 + n)
            elif kind == "down" and n < ND:
                eng.wait_ge(ffn_full, 2 * FT)
            elif kind == "down":
                eng.wait_ge(down_used, n - ND + 1)

        def split_hi(eng, s):
            if s % 2 == 0:
                eng.wait_ge(raw_in[s // 2 % 2], 32 * (s // 4 + 1))
            wait_split_free(eng, s)
            eng.activation(split_at(s)[0], raw_view(s), ACT.Copy).then_inc(weights_hi, 1)

        def split_lo(eng, s):
            eng.wait_ge(weights_hi, s + 1)
            hi, lo = split_at(s)
            eng.tensor_tensor(lo, raw_view(s), hi.bitcast(F32), ALU.subtract).then_inc(weights_split, 1)

        def stream_upto(step):
            return at_stream[("step", min(step + 2, NS - 1))] + 1

        def unit_of(u):
            if u < A_UNITS:
                return "a", u // NC_, u % NC_
            return "x", (u - A_UNITS) // 2, (u - A_UNITS) % 2

        def o_at(u, hi):
            kind, a, b = unit_of(u)
            if kind == "a":
                return (oa_hi if hi else oa_lo)[:, 4 * a:4 * a + 4, CHUNK * b:CHUNK * b + CHUNK]
            return (ox_hi if hi else ox_lo)[:, a, 2 * P * b:2 * P * b + 2 * P]

        def o_psum(u):
            v = bk(7)[:, 0:2 * P]
            return v.rearrange("p (j q) -> p j q", j=4) if u < A_UNITS else v

        def turned_at(e, hi):
            t, h = (e // 2, e % 2) if e < 2 * MT else (e // 2 - MT, e % 2)
            dst = ((memT_hi, memT_lo) if e < 2 * MT else (hT_hi, hT_lo))[0 if hi else 1]
            return dst[:, 4 * h:4 * h + 4, P * t:P * t + P]

        def as4(v):
            return v.rearrange("p (j q) -> p j q", j=4)

        E_MEM, E_X = 2 * MT, 2 * MT + 2 * TT
        E_MV, E_V = E_X + 2, E_X + 4
        block = ctx.enter_context(nc.Block())

        @block.sync
        def _(sp):
            chunks = len(stream) // 2

            def load_chunk(c):
                if c >= 2:
                    sp.wait_ge(weights_split, 2 * c - 2)
                for h, src in enumerate(chunk_halves(stream[2 * c])):
                    dst = raw[c % 2][:, h, :]
                    if len(src.shape) == 3:
                        dst = dst.rearrange("p (k n) -> p k n", k=4)
                    sp.dma_start(dst, src).then_inc(raw_in[c % 2], 16)

            for m in range(MT):
                sp.dma_start(mem_in[:, m, :], mem[P * m:P * m + P, :]).then_inc(mem_loaded[m], 16)
            sp.dma_start(g_mem_b[:, :], row_bcast(g_mem)).then_inc(gain_loaded["mem"], 16)
            load_chunk(0)
            for t in range(TT):
                sp.dma_start(x_in[:, t, :], x[P * t:P * t + P, :]).then_inc(x_loaded[t], 16)
            sp.dma_start(g_mix_pre_b[:, :], row_bcast(g_mix_pre)).then_inc(gain_loaded["pre"], 16)
            load_chunk(1)
            sp.wait_ge(rel_built, 1)
            sp.dma_start(rel_dram, rel_row[:, :]).then_inc(rel_saved, 16)
            load_chunk(2)
            sp.wait_ge(rel_saved, 16)
            for half in range(2):
                for g in range(GROUPS):
                    for pr in range(4):
                        head = 8 * g + 4 * (pr % 2) + pr // 2 + 2 * half
                        sp.dma_start(bias_back[64 * half:64 * half + 64, g, pr, :],
                                     ap(rel_dram, 192 * head, [[1, CHUNK], [1, KEYS]]))\
                          .then_inc(bias_loaded, 16)
            last_out = at_stream[("out", KT - 1)] // 2
            for c in range(3, chunks):
                load_chunk(c)
                if c == last_out:
                    sp.wait_ge(tile_full, len(tiles))
                    for t in range(TT):
                        sp.dma_start(x1[:, t, :], x[P * t:P * t + P, :]).then_inc(x_again[t], 16)
                    sp.dma_start(g_post_b[:, :], row_bcast(g_mix_post)).then_inc(gain_loaded["post"], 16)
                    sp.dma_start(g_ffn_pre_b[:, :], row_bcast(g_ffn_pre)).then_inc(gain_loaded["ffn_pre"], 16)
                if c == at_stream[("ffn", 20)] // 2:
                    sp.wait_ge(h2_ready, TT)
                    sp.dma_start(g_post_b[:, :], row_bcast(g_ffn_post)).then_inc(gain_loaded["ffn_post"], 16)
            for t in range(TT):
                sp.wait_ge(result_ready, t + 1)
                sp.dma_start(out[P * t:P * t + P, :], x1[:, t, :]).then_inc(stored, 16)
            sp.wait_ge(stored, 16 * TT)

        @block.gpsimd
        def _(pool):
            pool.memset(ident[:, :], 0.0).then_inc(pool_chain, 1)
            pool.memset(minus_half[:, :], -0.5).then_inc(consts_ready, 1)
            for i in range(PAD):
                pool.memset(inv_count[:, i:i + 1], 1.0 / (i + 1)).then_inc(consts_ready, 1)
            pool.wait_ge(pool_chain, 1)
            pool.affine_select(out=ident[:, :], in_=ident[:, :], compare_op=ALU.not_equal, fill=1.0, base=0,
                               pattern=[[-1, P]], channel_multiplier=1).then_inc(consts_ready, 1)
            pool.memset(k_dup[:, :, 0:CHUNK], 0.0).then_inc(pads_ready, 1)
            pool.memset(vT[:, 0:CHUNK], 0.0).then_inc(pads_ready, 1)
            pool.wait_ge(consts_ready, PAD + 2)
            chain = [1]

            def link(ins):
                chain[0] += 1
                ins.then_inc(pool_chain, 1)
                pool.wait_ge(pool_chain, chain[0])

            def inverse_rms(n):
                pool.wait_ge(squares_summed, n + 1)
                link(pool.tensor_scalar(meansq[:, n:n + 1], sumsq[:, n:n + 1], 1.0 / D, EPS, ALU.mult, ALU.add))
                pool.tensor_tensor(rstd[:, n:n + 1], meansq[:, n:n + 1], minus_half[:, :], ALU.pow)\
                    .then_inc(rstd_ready, 1)

            for n in range(MT + TT):
                inverse_rms(n)

            pool.wait_ge(rows_turned, E_V)
            for i in range(4):
                pool.memset(pooled[i][:, 0:PAD], 0.0).then_inc(pads_ready, 1)
            pool.wait_ge(pads_ready, 6)
            for g, w in enumerate(POOL_WINDOWS):
                src = pooled[g % 2]
                pool.wait_ge(tile_copied, copied_no[("pin", g)])
                if g >= 1:
                    pool.wait_ge(tile_full, tile_no[("map", g - 1)] + 1)
                cur, d, n = src, 1, 0
                while d < w:
                    nxt = pooled[2 + n % 2]
                    link(pool.tensor_tensor(nxt[:, PAD:], cur[:, PAD:], cur[:, PAD - d:PAD + SEQ - d], ALU.add))
                    cur, d, n = nxt, 2 * d, n + 1
                diff = pooled[2 + n % 2]
                link(pool.tensor_scalar(diff[:, PAD:], cur[:, PAD:], 1.0 / w, 0.0, ALU.mult, ALU.add))
                link(pool.tensor_tensor(diff[:, PAD:PAD + w - 1], cur[:, PAD:PAD + w - 1], inv_count[:, 0:w - 1], ALU.mult))
                pool.tensor_tensor(diff[:, PAD:], diff[:, PAD:], src[:, PAD:], ALU.subtract).then_inc(pool_diff_ready, 1)

            for n in range(NORM_MIX, NORM_MIX + 3 * TT):
                inverse_rms(n)

        def diff_at(g):
            return pooled[2 + (g + 1) % 2]

        @block.scalar
        def _(act):
            act.dma_start(relT[:, :], rel_bias).then_inc(rel_loaded, 16)
            for half in range(2):
                act.dma_start(sink[64 * half:64 * half + 64, :, :], ap(sinks, 8 * half, [[0, 64], [4, 2], [1, 4]]))\
                   .then_inc(smalls_loaded, 16)
            act.dma_start(scale_p[:, :], pool_scale).then_inc(smalls_loaded, 16)
            act.dma_start(w_map[:, :, :], w_pool_map.rearrange("g c d -> c g d")).then_inc(smalls_loaded, 16)

            def sum_squares(src, n, scratch):
                act.activation(scratch, src, ACT.Square, accum_out=sumsq[:, n:n + 1]).then_inc(squares_summed, 1)
                act.wait_ge(squares_summed, n + 1)

            def turn_hi(e):
                act.wait_ge(rows_turned, e + 1)
                act.activation(turned_at(e, True), as4(bk(4 + e % 4)), ACT.Copy).then_inc(turned_hi, 1)

            def probsT_copy(u):
                act.wait_ge(probs_turned, u + 1)
                if u >= 1:
                    act.wait_ge(o_full, u)
                act.activation(probsT[:, :, :], as4(bk(6)), ACT.Copy).then_inc(probsT_ready, 1)

            def exps(u):
                kind, a, b = unit_of(u)
                act.wait_ge(neg_max_ready, u + 1)
                pr = probs[u % 2]
                if kind == "a":
                    for i in range(4):
                        act.activation(pr[:, i, :], pr[:, i, :], ACT.Exp, bias=neg_max[u % 2][:, i:i + 1],
                                       accum_out=row_sum[u % 2][:, i:i + 1])
                    act.activation(sink_gap[u % 2][:, :], sink_gap[u % 2][:, :], ACT.Exp).then_inc(exps_done, 1)
                else:
                    act.wait_ge(probs_turned, u - 1)
                    flat = pr[:, :, :].rearrange("p (t m) k -> p t (m k)", t=2)
                    for i in range(2):
                        ins = act.activation(flat[:, i, :], scores[:, i, 0:N_MEM], ACT.Exp,
                                             bias=neg_max[u % 2][:, i:i + 1], scale=X_SCALE,
                                             accum_out=row_sum[u % 2][:, i:i + 1])
                    ins.then_inc(exps_done, 1)

            def o_hi(u):
                act.wait_ge(o_full, u + 1)
                act.activation(o_at(u, True), o_psum(u), ACT.Copy).then_inc(o_hi_done, 1)

            def take(t):
                kind, i = t
                n = tile_no[t]
                src = bk(n % 4)
                act.wait_ge(tile_full, n + 1)
                if kind == "mem":
                    dst = mk[:, i, :] if i < X_HEADS else mvT[:, i - X_HEADS, :]
                    act.activation(dst, src[:, 0:N_MEM], ACT.Copy).then_inc(tile_copied, 1)
                elif kind == "k":
                    act.wait_ge(pads_ready, 2)
                    for g in range(GROUPS):
                        for half in range(2):
                            ins = act.activation(k_dup[64 * half:64 * half + 64, g, CHUNK:],
                                                 src[64 * g:64 * g + 64, :], ACT.Copy)
                    ins.then_inc(tile_copied, 1)
                elif kind == "v":
                    act.activation(vT[:, CHUNK:], src, ACT.Copy).then_inc(tile_copied, 1)
                elif kind == "q":
                    act.activation(q[:, i // 2, :, i % 2, :], src.rearrange("p (c t) -> p c t", c=NC_), ACT.Copy)\
                        .then_inc(tile_copied, 1)
                elif kind == "qx":
                    act.activation(qx[:, i, :], src, ACT.Copy).then_inc(tile_copied, 1)
                elif kind == "pin":
                    if i >= 2:
                        act.wait_ge(pool_diff_ready, i - 1)
                    act.wait_ge(rows_turned, E_V)
                    act.activation(pooled[i % 2][:, PAD:], src, ACT.Copy).then_inc(tile_copied, 1)
                elif kind == "gate":
                    if i >= 12:
                        act.wait_ge(mrg_split, 2 * (i // 6) - 2)
                    act.activation(gates[:, i % 12, :], src, ACT.Copy).then_inc(tile_copied, 1)
                elif kind == "map":
                    act.activation(op_hi[:, i, :], src, ACT.Copy, scale=scale_p[:, i:i + 1]).then_inc(map_hi_done, 1)

            def sigmoids(j):
                for b in range(3):
                    i = 6 * (j // 2) + 2 * b + j % 2
                    act.wait_ge(tile_copied, copied_no[("gate", i)])
                    v = gates[:, i % 12, :]
                    act.activation(v, v, ACT.Sigmoid).then_inc(sigmoid_ready, 1)

            def merged_hi(j):
                act.wait_ge(mixed_ready, j + 1)
                act.activation(mrg_hi[:, j, :], mixed[j % 2][:, :], ACT.Copy).then_inc(mrg_hi_done, 1)

            for m in range(MT):
                act.wait_ge(mem_loaded[m], 16)
                sum_squares(mem_in[:, m, :], NORM_MEM + m, square0[:, :])
            for s in range(2):
                split_hi(act, s)
            for e in range(E_MEM):
                turn_hi(e)
            for t in range(TT):
                act.wait_ge(x_loaded[t], 16)
                sum_squares(x_in[:, t, :], NORM_X + t, square0[:, :])

            done = 2
            for s in range(NS):
                u = s - UNIT0
                if 0 <= u - 2 < UNITS:
                    o_hi(u - 2)
                if s >= 2 and steps[s - 2][0][0] == "p":
                    merged_hi(steps[s - 2][0][1])
                while done < stream_upto(s):
                    split_hi(act, done)
                    done += 1
                if 0 <= u - 1 < UNITS:
                    probsT_copy(u - 1)
                if s >= 1:
                    for t in steps[s - 1]:
                        if t in copied_no or t[0] == "map":
                            take(t)
                if 1 <= s < 5:
                    for e in range(E_MEM + 2 * (s - 1), E_MEM + 2 * s):
                        turn_hi(e)
                if 0 <= u < UNITS:
                    exps(u)
                if steps[s][0][0] == "a":
                    sigmoids(steps[s][0][1])
            for j in (KT - 2, KT - 1):
                merged_hi(j)

            def h2_hi(t):
                for h in range(2):
                    act.wait_ge(rows_turned, E_V + 2 * t + h + 1)
                    act.activation(h2T_hi[:, 4 * h:4 * h + 4, P * t:P * t + P], as4(bk(2 * t + h)), ACT.Copy)\
                        .then_inc(turned_hi, 1)

            n_out = at_stream[("ffn", 0)]
            while done < n_out:
                split_hi(act, done)
                done += 1
            for t in range(TT):
                if t >= 1:
                    h2_hi(t - 1)
                act.wait_ge(out_full, t + 1)
                sum_squares(row_banks(t), NORM_MIX + 2 * t, square1[:, :])
                if t < 3:
                    split_hi(act, done)
                    done += 1
                act.wait_ge(x1_ready, t + 1)
                sum_squares(x1[:, t, :], NORM_MIX + 2 * t + 1, square1[:, :])
            split_hi(act, done)
            done += 1
            h2_hi(TT - 1)

            for e in range(2 * FT):
                f, i = divmod(e, 4)
                act.wait_ge(ffn_full, e + 1)
                split_hi(act, done)
                done += 1
                if i < 2:
                    if f >= 1:
                        act.wait_ge(prod_ready, 2 * f - 1 + i)
                    act.activation(silu[i][:, :], bk(i), ACT.Silu).then_inc(silu_ready, 1)
                else:
                    n = 2 * f + i - 2
                    act.wait_ge(prod_ready, n + 1)
                    act.activation(f_hi[:, n, :], prod[i - 2][:, :], ACT.Copy).then_inc(f_hi_done, 1)
            while done < len(stream):
                split_hi(act, done)
                done += 1
            for t in range(TT):
                act.wait_ge(down_full, t + 1)
                sum_squares(row_banks(t), NORM_POST + t, square1[:, :])

        @block.vector
        def _(dve):
            chain = [0]

            def link(ins):
                chain[0] += 1
                ins.then_inc(vec_chain, 1)
                dve.wait_ge(vec_chain, chain[0])

            dve.wait_ge(rel_loaded, 16)
            ranges = bucket_ranges()
            for n, (a, b, bucket) in enumerate(ranges):
                ins = dve.tensor_copy(rel_row[:, a:b], relT[:, bucket:bucket + 1].to_broadcast([A_HEADS, b - a]))
                if n == len(ranges) - 1:
                    ins = dve.memset(rel_row[:, b:192], 0.0)
            ins.then_inc(rel_built, 1)

            def norm_rows(src, n, gain):
                dve.wait_ge(rstd_ready, n + 1)
                dve.scalar_tensor_tensor(out=src, in0=src, scalar=rstd[:, n:n + 1], in1=gain, op0=ALU.mult,
                                         op1=ALU.mult).then_inc(rows_normed, 1)

            def turn_lo(e):
                dve.wait_ge(turned_hi, e + 1)
                dve.tensor_tensor(turned_at(e, False), as4(bk(4 + e % 4)), turned_at(e, True).bitcast(F32),
                                  ALU.subtract).then_inc(turned_split, 1)

            def maxima(u):
                kind, a, b = unit_of(u)
                pr, mx = probs[u % 2], row_max[u % 2]
                dve.wait_ge(scores_full, u + 1)
                if kind == "a":
                    if u == 0:
                        dve.wait_ge(bias_loaded, 16 * 16)
                        v = bias_back[:, :, :, :]
                        back = bass.AP(v.tensor, v.offset + KEYS - 1, [list(v.ap[0]), [KEYS, 4 * GROUPS], [-1, KEYS]])
                        link(dve.tensor_copy(bias[:, :, :, :].rearrange("p g a k -> p (g a) k"), back))
                        dve.wait_ge(smalls_loaded, 16 * 4)
                    if u >= 2:
                        dve.wait_ge(probs_turned, u - 1)
                    dve.scalar_tensor_tensor(out=pr[:, :, :].rearrange("p (a b) k -> p a b k", a=2),
                                             in0=scores[:, :, 0:2 * KEYS].rearrange("p a (b k) -> p a b k", b=2),
                                             scalar=A_SCALE,
                                             in1=bias[:, a, :, :].rearrange("p (a b) k -> p a b k", a=2),
                                             op0=ALU.mult, op1=ALU.add).then_inc(scores_read, 1)
                    dve.wait_ge(scores_read, u + 1)
                    if b == 0:
                        link(dve.memset(pr[:, :, 0:CHUNK], -1e30))
                    link(dve.tensor_reduce(mx[:, :], pr[:, :, :], AX_X, ALU.max))
                    link(dve.tensor_tensor(mx[:, :], mx[:, :], sink[:, a, :], ALU.max))
                    dve.tensor_tensor(sink_gap[u % 2][:, :], sink[:, a, :], mx[:, :], ALU.subtract)
                    dve.tensor_scalar(neg_max[u % 2][:, :], mx[:, :], -1.0, None, ALU.mult).then_inc(neg_max_ready, 1)
                else:
                    link(dve.tensor_reduce(mx[:, 0:2], scores[:, :, 0:N_MEM], AX_X, ALU.max))
                    dve.tensor_scalar(neg_max[u % 2][:, 0:2], mx[:, 0:2], -X_SCALE, None, ALU.mult)\
                       .then_inc(neg_max_ready, 1)

            def normalise(u):
                kind, a, b = unit_of(u)
                pr, r = probs[u % 2], inv_denom[u % 2]
                dve.wait_ge(exps_done, u + 1)
                if kind == "a":
                    link(dve.tensor_tensor(denom[u % 2][:, :], row_sum[u % 2][:, :], sink_gap[u % 2][:, :], ALU.add))
                    link(dve.reciprocal(r[:, :], denom[u % 2][:, :]))
                    v, n, w = pr[:, :, :], 4, KEYS
                else:
                    link(dve.reciprocal(r[:, 0:2], row_sum[u % 2][:, 0:2]))
                    v, n, w = pr[:, :, :].rearrange("p (t m) k -> p t (m k)", t=2), 2, N_MEM
                dve.tensor_tensor(v, v, r[:, 0:n].unsqueeze(2).to_broadcast([P, n, w]), ALU.mult)\
                   .then_inc(probs_ready, 1)

            def o_lo(u):
                dve.wait_ge(o_hi_done, u + 1)
                dve.tensor_tensor(o_at(u, False), o_psum(u), o_at(u, True).bitcast(F32), ALU.subtract)\
                   .then_inc(o_split, 1)

            def map_lo(g):
                dve.wait_ge(map_hi_done, g + 1)
                dve.scalar_tensor_tensor(out=op_lo[:, g, :], in0=bk(tile_no[("map", g)] % 4), scalar=scale_p[:, g:g + 1],
                                         in1=op_hi[:, g, :].bitcast(F32), op0=ALU.mult, op1=ALU.subtract)\
                   .then_inc(tile_merged, 1)

            def merge(t):
                kind, j = t
                n = tile_no[t]
                b = "axp".index(kind)
                gate = gates[:, (6 * (j // 2) + 2 * b + j % 2) % 12, :]
                dve.wait_ge(tile_full, n + 1)
                dve.wait_ge(sigmoid_ready, 3 * j + 3)
                if kind == "p" and j >= 1:
                    dve.wait_ge(mixed_ready, j)
                dst = mixed[j % 2] if kind == "a" else part
                dve.tensor_tensor(dst[:, :], bk(n % 4), gate, ALU.mult).then_inc(tile_merged, 1)
                dve.wait_ge(tile_merged, merged_no[t])
                if kind != "a":
                    ins = dve.tensor_tensor(mixed[j % 2][:, :], mixed[j % 2][:, :], part[:, :], ALU.add)
                    if kind == "p":
                        link(ins)
                    else:
                        ins.then_inc(mixed_ready, 1)

            def merged_lo(j):
                dve.wait_ge(mrg_hi_done, j + 1)
                dve.tensor_tensor(mrg_lo[:, j, :], mixed[j % 2][:, :], mrg_hi[:, j, :].bitcast(F32), ALU.subtract)\
                   .then_inc(mrg_split, 1)
                dve.wait_ge(mrg_split, j + 1)

            dve.wait_ge(gain_loaded["mem"], 16)
            for m in range(MT):
                norm_rows(mem_in[:, m, :], NORM_MEM + m, g_mem_b[:, :])
            for s in range(2):
                split_lo(dve, s)
            for e in range(E_MEM):
                turn_lo(e)
            dve.wait_ge(gain_loaded["pre"], 16)
            for t in range(TT):
                norm_rows(x_in[:, t, :], NORM_X + t, g_mix_pre_b[:, :])

            done = 2
            for s in range(NS):
                u = s - UNIT0
                if 0 <= u - 2 < UNITS:
                    o_lo(u - 2)
                if s >= 2 and steps[s - 2][0][0] == "p":
                    merged_lo(steps[s - 2][0][1])
                if 0 <= u < UNITS:
                    maxima(u)
                while done < stream_upto(s):
                    split_lo(dve, done)
                    done += 1
                if s >= 1:
                    for t in steps[s - 1]:
                        if t[0] == "map":
                            map_lo(t[1])
                        elif t[0] in "axp":
                            merge(t)
                if 1 <= s < 5:
                    for e in range(E_MEM + 2 * (s - 1), E_MEM + 2 * s):
                        turn_lo(e)
                if s == 10:
                    for e in range(E_X, E_V):
                        dve.wait_ge(rows_turned, e + 1)
                        if e < E_MV:
                            dst = mv[:, e - E_X, :, :]
                        else:
                            dst = v_c[:, 4 * (e - E_MV):4 * (e - E_MV) + 4, :]
                        dve.tensor_copy(dst, as4(bk(4 + e % 4))).then_inc(turned_split, 1)
                if 0 <= u < UNITS:
                    normalise(u)
            for t in steps[NS - 1]:
                merge(t)
            for j in (KT - 2, KT - 1):
                merged_lo(j)

            def post_norm(t, n, ready, full):
                dve.wait_ge(rstd_ready, n + 1)
                link(dve.scalar_tensor_tensor(out=y[t % 2][:, :], in0=row_banks(t), scalar=rstd[:, n:n + 1],
                                              in1=g_post_b[:, :], op0=ALU.mult, op1=ALU.mult))
                dve.tensor_tensor(x1[:, t, :], x1[:, t, :], y[t % 2][:, :], ALU.add).then_inc(ready, 1)

            def h2_lo(t):
                for h in range(2):
                    e = 2 * t + h
                    dve.wait_ge(turned_hi, E_X + e + 1)
                    dst = (slice(None), slice(4 * h, 4 * h + 4), slice(P * t, P * t + P))
                    dve.tensor_tensor(h2T_lo[dst], as4(bk(2 * t + h)), h2T_hi[dst].bitcast(F32), ALU.subtract)\
                       .then_inc(turned_split, 1)

            while done < at_stream[("ffn", 0)]:
                split_lo(dve, done)
                done += 1
            dve.wait_ge(gain_loaded["post"], 16)
            dve.wait_ge(gain_loaded["ffn_pre"], 16)
            for t in range(TT):
                if t >= 1:
                    h2_lo(t - 1)
                dve.wait_ge(x_again[t], 16)
                if t >= 2:
                    dve.wait_ge(rows_turned, E_V + 2 * t - 2)
                post_norm(t, NORM_MIX + 2 * t, x1_ready, out_full)
                if t < 3:
                    split_lo(dve, done)
                    done += 1
                n = NORM_MIX + 2 * t + 1
                dve.wait_ge(rstd_ready, n + 1)
                dve.scalar_tensor_tensor(out=y[t % 2][:, :], in0=x1[:, t, :], scalar=rstd[:, n:n + 1],
                                         in1=g_ffn_pre_b[:, :], op0=ALU.mult, op1=ALU.mult).then_inc(h2_ready, 1)
            split_lo(dve, done)
            done += 1
            h2_lo(TT - 1)

            for e in range(2 * FT):
                f, i = divmod(e, 4)
                dve.wait_ge(ffn_full, e + 1)
                if i >= 2:
                    n = 2 * f + i - 2
                    dve.wait_ge(silu_ready, n + 1)
                    dve.tensor_tensor(prod[i - 2][:, :], silu[i - 2][:, :], bk(i), ALU.mult).then_inc(prod_ready, 1)
                split_lo(dve, done)
                done += 1
                if i >= 2:
                    dve.wait_ge(f_hi_done, n + 1)
                    dve.tensor_tensor(f_lo[:, n, :], prod[i - 2][:, :], f_hi[:, n, :].bitcast(F32), ALU.subtract)\
                       .then_inc(f_split, 1)
                    dve.wait_ge(f_split, n + 1)
            while done < len(stream):
                split_lo(dve, done)
                done += 1
            dve.wait_ge(gain_loaded["ffn_post"], 16)
            for t in range(TT):
                post_norm(t, NORM_POST + t, result_ready, down_full)

        @block.tensor
        def _(pe):
            def three(dst, whi, wlo, xhi, xlo, first, last, swap=False):
                pairs = [(whi, xhi), (whi, xlo), (wlo, xhi)]
                if swap:
                    pairs = [(xhi, whi), (xhi, wlo), (xlo, whi)]
                for n, (a, b) in enumerate(pairs):
                    ins = pe.matmul(dst, a, b, start=first and n == 0, stop=last and n == 2)
                return ins

            def turn_rows(src, e):
                if E_MEM <= e:
                    pe.wait_ge(turned_split, e - 3)
                for i in range(4):
                    ins = pe.transpose(bk(4 + e % 4)[:, P * i:P * i + P], src[:, P * i:P * i + P], ident[:, :])
                ins.then_inc(rows_turned, 1)

            def tile(t, s):
                kind, i = t
                n = tile_no[t]
                dst = bk(n % 4)
                if n >= 4:
                    before = tiles[n - 4]
                    if before in copied_no:
                        pe.wait_ge(tile_copied, copied_no[before])
                    else:
                        pe.wait_ge(tile_merged, merged_no[before])
                if kind == "map":
                    pe.wait_ge(pool_diff_ready, i + 1)
                    pe.matmul(dst, w_map[:, i, :], diff_at(i)[:, PAD:], start=True, stop=True).then_inc(tile_full, 1)
                    return
                whi, wlo = w_hi[s % 3], w_lo[s % 3]
                pe.wait_ge(weights_split, at_stream[("step", s)] + 1)
                if kind == "mem":
                    xhi, xlo, dst = memT_hi, memT_lo, dst[:, 0:N_MEM]
                elif kind in ("a", "p", "x"):
                    xhi, xlo = {"a": (oa_hi, oa_lo), "p": (op_hi, op_lo), "x": (ox_hi, ox_lo)}[kind]
                else:
                    xhi, xlo = hT_hi, hT_lo
                if kind == "mem" and i == 0:
                    pe.wait_ge(turned_split, E_MEM)
                if kind == "k":
                    pe.wait_ge(turned_split, E_X)
                if kind == "a":
                    pe.wait_ge(o_split, A_UNITS)
                if kind == "p":
                    pe.wait_ge(tile_merged, merged_no[("map", 3)])
                if kind == "x":
                    pe.wait_ge(o_split, UNITS)
                ks = {"p": range(4), "x": range(4, 8)}.get(kind, range(8))
                for k in ks:
                    kx = k - 4 if kind == "x" else k
                    ins = three(dst, whi[:, k, :], wlo[:, k, :], xhi[:, kx, :], xlo[:, kx, :],
                                k == ks[0], k == ks[-1])
                ins.then_inc(tile_full, 1)

            def unit_scores(u):
                kind, a, b = unit_of(u)
                if u >= 1:
                    pe.wait_ge(scores_read if u <= A_UNITS else exps_done, u)
                else:
                    pe.wait_ge(turned_split, E_V)
                if kind == "a":
                    pe.wait_ge(tile_copied, copied_no[("q", 4 * a + 3)])
                    for pr in range(4):
                        lo = 64 * (pr // 2)
                        ins = pe.matmul(scores[:, pr // 2, KEYS * (pr % 2):KEYS * (pr % 2) + KEYS],
                                        q[lo:lo + 64, 2 * a + pr % 2, b, :, :].rearrange("p j t -> p (j t)"),
                                        k_dup[lo:lo + 64, a, CHUNK * b:CHUNK * b + KEYS], start=True, stop=True)
                else:
                    pe.wait_ge(tile_copied, copied_no[("qx", a)])
                    for i in range(2):
                        at = P * (2 * b + i)
                        ins = pe.matmul(scores[:, i, 0:N_MEM], qx[:, a, at:at + P], mk[:, a, :], start=True, stop=True)
                ins.then_inc(scores_full, 1)

            def unit_turn(u):
                pe.wait_ge(probs_ready, u + 1)
                if u >= 1:
                    pe.wait_ge(probsT_ready, u)
                for i in range(4):
                    dst = i if u < A_UNITS else 2 * (i % 2) + i // 2
                    ins = pe.transpose(bk(6)[:, P * dst:P * dst + P], probs[u % 2][:, i, :], ident[:, :])
                ins.then_inc(probs_turned, 1)

            def unit_out(u):
                kind, a, b = unit_of(u)
                pe.wait_ge(probsT_ready, u + 1)
                if u >= 1:
                    pe.wait_ge(o_split, u)
                if kind == "a":
                    for half in range(2):
                        ins = pe.matmul(bk(7)[64 * half:64 * half + 64, 0:2 * P], v_c[:, b, 64 * a:64 * a + 64],
                                        probsT[:, 2 * half:2 * half + 2, :], start=True, stop=True)
                else:
                    for m in range(MT):
                        ins = pe.matmul(bk(7)[:, 0:2 * P], mv[:, m, a, :], probsT[:, 2 * m:2 * m + 2, :],
                                        start=(m == 0), stop=(m == MT - 1))
                ins.then_inc(o_full, 1)

            pe.wait_ge(consts_ready, PAD + 2)
            for m in range(MT):
                pe.wait_ge(rows_normed, m + 1)
                for h in range(2):
                    turn_rows(mem_in[:, m, 512 * h:512 * h + 512], 2 * m + h)
            for s in range(NS):
                u = s - UNIT0
                if 0 <= u < UNITS:
                    unit_scores(u)
                if 0 <= u - 1 < UNITS:
                    unit_turn(u - 1)
                for t in steps[s]:
                    tile(t, s)
                if 0 <= u - 1 < UNITS:
                    unit_out(u - 1)
                if s < TT:
                    pe.wait_ge(rows_normed, MT + s + 1)
                    for h in range(2):
                        turn_rows(x_in[:, s, 512 * h:512 * h + 512], E_MEM + 2 * s + h)
                if s == 9:
                    pe.wait_ge(tile_copied, copied_no[("v", 0)])
                    for m in range(MT):
                        e = E_X + m
                        pe.wait_ge(turned_split, e - 3)
                        for h in range(X_HEADS):
                            ins = pe.transpose(bk(4 + e % 4)[:, P * h:P * h + P], mvT[:, h, P * m:P * m + P], ident[:, :])
                        ins.then_inc(rows_turned, 1)
                    for half in range(2):
                        e = E_MV + half
                        pe.wait_ge(turned_split, e - 3)
                        for i in range(4):
                            c = 4 * half + i
                            ins = pe.transpose(bk(4 + e % 4)[:, P * i:P * i + P], vT[:, CHUNK * c:CHUNK * c + P], ident[:, :])
                        ins.then_inc(rows_turned, 1)

            def turn_h2(t):
                pe.wait_ge(h2_ready, t + 1)
                for h in range(2):
                    for i in range(4):
                        at = P * (4 * h + i)
                        ins = pe.transpose(bk(2 * t + h)[:, P * i:P * i + P], y[t % 2][:, at:at + P], ident[:, :])
                    ins.then_inc(rows_turned, 1)

            for t in range(TT):
                if t < 2:
                    pe.wait_ge(tile_merged, merged_no[tiles[-1]])
                for k in range(KT):
                    if t == 0:
                        pe.wait_ge(weights_split, at_stream[("out", k)] + 1)
                        pe.wait_ge(mrg_split, k + 1)
                    for h in range(2):
                        ins = three(bk(2 * t + h), wo_hi[k][:, 512 * h:512 * h + 512], wo_lo[k][:, 512 * h:512 * h + 512],
                                    mrg_hi[:, k, P * t:P * t + P], mrg_lo[:, k, P * t:P * t + P],
                                    k == 0, k == KT - 1, swap=True)
                    if t == TT - 1 and k == 5:
                        turn_h2(TT - 2)
                ins.then_inc(out_full, 1)
                if 1 <= t < TT - 1:
                    turn_h2(t - 1)

            def ffn_part(e, lo, hi):
                for k in range(KT):
                    ins = three(bk(e % 4)[:, lo:hi], w_hi[e % 4][:, k, :], w_lo[e % 4][:, k, :],
                                h2T_hi[:, k, lo:hi], h2T_lo[:, k, lo:hi], k == 0, k == KT - 1)
                return ins

            EARLY = 3
            for e in range(EARLY):
                pe.wait_ge(weights_split, at_stream[("ffn", e)] + 1)
                pe.wait_ge(turned_split, E_V + 6)
                ffn_part(e, 0, 3 * P)
            turn_h2(TT - 1)
            pe.wait_ge(turned_split, E_V + 8)
            for e in range(EARLY):
                ffn_part(e, 3 * P, SEQ).then_inc(ffn_full, 1)
            for e in range(EARLY, 2 * FT):
                f, i = divmod(e, 4)
                pe.wait_ge(weights_split, at_stream[("ffn", e)] + 1)
                if f >= 1:
                    pe.wait_ge(silu_ready if i < 2 else prod_ready, 2 * f - 1 + i % 2)
                ffn_part(e, 0, SEQ).then_inc(ffn_full, 1)

            def down(t, k, inc=None):
                s = k % ND
                for h in range(2):
                    ins = three(bk(2 * t + h), wd_hi[s][:, 512 * h:512 * h + 512], wd_lo[s][:, 512 * h:512 * h + 512],
                                f_hi[:, k, P * t:P * t + P], f_lo[:, k, P * t:P * t + P],
                                k == 0, k == FT - 1, swap=True)
                return ins

            TAIL = 8
            pe.wait_ge(turned_split, E_V + 8)
            for k in range(FT - TAIL):
                pe.wait_ge(weights_split, at_stream[("down", k)] + 1)
                pe.wait_ge(f_split, k + 1)
                for t in (2, 3, 0, 1):
                    if k == 0 and t == 0:
                        pe.wait_ge(silu_ready, FT)
                        pe.wait_ge(prod_ready, FT)
                    ins = down(t, k)
                ins.then_inc(down_used, 1)
            for t in range(TT):
                for k in range(FT - TAIL, FT):
                    if t == 0:
                        pe.wait_ge(weights_split, at_stream[("down", k)] + 1)
                        pe.wait_ge(f_split, k + 1)
                    ins = down(t, k)
                ins.then_inc(down_full, 1)


_INS = ["x", "mem", "norm_mix_pre", "norm_mix_post", "norm_mem", "w_in", "rel_bias", "attn_sinks", "w_mem_kv",
        "w_pool_map", "pool_scale", "w_branch_a", "w_branch_x", "w_branch_p", "w_out", "norm_ffn_pre",
        "norm_ffn_post", "w_ffn_gate", "w_ffn_up", "w_ffn_down"]


def kernel(**inputs):
    import concourse.bacc as bacc
    from concourse.bass_utils import run_bass_kernel_spmd

    nc = bacc.Bacc("TRN2", target_bir_lowering=False, num_devices=1)
    arrays, args = {}, []
    for name in _INS:
        a = np.ascontiguousarray(inputs[name])
        if name != "rel_bias":
            a = a[0]
        if name == "rel_bias":
            a = a.T
        elif name == "pool_scale":
            a = a.reshape(4, P).T
        elif name == "attn_sinks":
            a = a.reshape(GROUPS, 2, 2, 2).transpose(2, 0, 3, 1)
        a = np.ascontiguousarray(a)
        arrays[f"in_{name}"] = a
        args.append(nc.dram_tensor(f"in_{name}", a.shape, mybir.dt.from_np(a.dtype), kind="ExternalInput").ap())
    result = nc.dram_tensor("result", (SEQ, D), F32, kind="ExternalOutput").ap()
    encoder_block(nc, *args, result)
    r = run_bass_kernel_spmd(nc, [arrays], core_ids=[0])
    return r.results[0]["result"].reshape(1, SEQ, D)
```

```python
import math
from contextlib import ExitStack

import numpy as np

import concourse.bass as bass
from concourse import mybir

F32 = mybir.dt.float32
F32R = mybir.dt.float32r
BF16 = mybir.dt.bfloat16
ALU = mybir.AluOpType
ACT = mybir.ActivationFunctionType
AX_X = mybir.AxisListType.X

P = 128
SEQ, D, N_MEM = 512, 1024, 256
TT, MT, KT = SEQ // P, N_MEM // P, D // P
CHUNK = 64
NC_ = SEQ // CHUNK
A_HEADS, HD, GROUPS = 16, 64, 2
KEYS = 2 * CHUNK
X_HEADS = 4
POOL_WINDOWS = (2, 4, 8, 16)
PAD = 16
D_FF = 2816
FT = D_FF // P
EPS = 1e-6
A_SCALE = float(HD) ** -0.5
X_SCALE = float(P) ** -0.5
REL_BUCKETS = 32

K_COL = A_HEADS * HD
V_COL = K_COL + P
QX_COL = V_COL + P
PIN_COL = QX_COL + X_HEADS * P
GATE_COL = PIN_COL + 4 * P

A_UNITS = GROUPS * NC_
X_UNITS = X_HEADS * 2
UNITS = A_UNITS + X_UNITS

KB = 1024
PAIR_OF = (2, 0, 1, 3)
WARM_UP = (30, 0, 3)
X_AFTER = (2, 3, 5, 6)
TAIL = 8


def bucket_ranges():
    rel = np.arange(-(KEYS - 1), CHUNK)[::-1]
    nb, n = REL_BUCKETS // 2, np.abs(rel)
    exact = nb // 2
    large = exact + (np.log(np.maximum(n, 1) / exact) / np.log(KEYS / exact) * (nb - exact)).astype(np.int32)
    ids = (rel > 0) * nb + np.where(n < exact, n, np.minimum(large, nb - 1))
    cuts = [0] + [i for i in range(1, len(ids)) if ids[i] != ids[i - 1]] + [len(ids)]
    return [(a, b, int(ids[a])) for a, b in zip(cuts, cuts[1:])]


def plan():
    steps = [[("mem", h)] for h in range(2 * X_HEADS)]
    steps += [[("k", 0)], [("v", 0)]]
    steps += [[("q", j)] for j in range(8)]
    steps += [[("qx", h)] for h in range(X_HEADS)]
    steps += [[("pin", g)] for g in range(4)]

    def gates(jp):
        return [[("gate", 6 * jp + 2 * b + i)] for b in range(3) for i in range(2)]

    def merge(jp):
        a = [[("a", 2 * jp)], [("a", 2 * jp + 1)]]
        return a + [[("p", j), ("x", j)] for j in (2 * jp, 2 * jp + 1)]

    steps += gates(0) + gates(1)
    steps += merge(0) + gates(2) + merge(1) + gates(3) + merge(2) + merge(3)
    first = steps.index([("pin", 0)])
    for g in range(4):
        steps[first + 3 + 2 * g].append(("map", g))
    n = len(steps)
    stream = [("step", s) for s in range(n)]
    for c, at in ((1, n - 2), (0, n - 6)):
        stream[at:at] = [("out", 2 * c), ("out", 2 * c + 1)]
    stream += [("out", k) for k in range(4, KT)]
    stream += [("ffn", e) for e in range(2 * FT)]
    stream += [("down", k) for k in range(FT)]
    return steps, stream


def encoder_block(nc, x, mem, g_mix_pre, g_mix_post, g_mem, w_in, rel_bias, sinks, w_mem_kv, w_pool_map,
                  pool_scale, w_branch_a, w_branch_x, w_branch_p, w_out, g_ffn_pre, g_ffn_post,
                  w_gate, w_up, w_down, out):
    steps, stream = plan()
    NS = len(steps)
    tiles = [t for s in steps for t in s]
    tile_no = {t: n for n, t in enumerate(tiles)}
    step_end = np.cumsum([len(s) for s in steps]).tolist()
    at_stream = {g: n for n, g in enumerate(stream)}
    UNIT0 = steps.index([("q", 5)])

    copied_kinds = ("mem", "k", "v", "q", "qx", "pin", "gate")
    copied_no, merged_no = {}, {}
    for t in tiles:
        d = copied_no if t[0] in copied_kinds else merged_no
        d[t] = len(d) + 1

    def ap(t, offset, pattern):
        return bass.AP(t.tensor, t.offset + offset, pattern)

    def row_bcast(v, n=D):
        return ap(v, 0, [[0, P], [1, n]])

    BASE = 16512

    def sb(name, kb, shape, dt=F32):
        return nc.alloc_sbuf_tensor_at(name, shape, dt, offset=BASE + int(kb * KB))

    raw = [sb(f"raw{i}", 8 * i, [P, 2, 1024]) for i in range(2)]
    narrow_at = [16, 24, 32, 196]
    w_hi = [sb(f"w_hi{i}", a, [P, 8, P], F32R) for i, a in enumerate(narrow_at)]
    w_lo = [sb(f"w_lo{i}", a + 4, [P, 8, P], F32R) for i, a in enumerate(narrow_at)]
    hT_hi, hT_lo = sb("hT_hi", 40, [P, KT, SEQ], F32R), sb("hT_lo", 56, [P, KT, SEQ], F32R)
    memT_hi, memT_lo = sb("memT_hi", 72, [P, KT, N_MEM], F32R), sb("memT_lo", 80, [P, KT, N_MEM], F32R)
    gates = sb("gates", 72, [P, 12, SEQ])
    k_dup = sb("k_dup", 96, [P, GROUPS, CHUNK + SEQ])
    v_c = sb("v_c", 100.5, [P, NC_, P])
    bias = sb("bias", 104.5, [P, GROUPS, 4, KEYS])
    mv = sb("mv", 108.5, [P, MT, X_HEADS, P])
    probs = [sb(f"probs{i}", 112.5 + 2 * i, [P, 4, P]) for i in range(2)]
    probsT = sb("probsT", 116.5, [P, 4, P])
    pooled = [sb(f"pooled{i}", 118.5 + 2.0625 * i, [P, PAD + SEQ]) for i in range(4)]
    vT = sb("vT", 118.5, [P, CHUNK + SEQ])
    mrg_hi, mrg_lo = sb("mrg_hi", 96, [P, KT, SEQ], F32R), sb("mrg_lo", 112, [P, KT, SEQ], F32R)
    oa_hi, oa_lo = sb("oa_hi", 128, [P, 8, SEQ], F32R), sb("oa_lo", 144, [P, 8, SEQ], F32R)
    x_in = sb("x_in", 128, [P, TT, D])
    mem_in = sb("mem_in", 144, [P, MT, D])
    square0 = sb("square0", 152, [P, D])
    g_mem_b = sb("g_mem_b", 156, [P, D])
    q = sb("q", 160, [P, 4, NC_, 2, CHUNK])
    g_mix_pre_b = sb("g_mix_pre_b", 172, [P, D])
    ox_hi, ox_lo = sb("ox_hi", 160, [P, 4, SEQ], F32R), sb("ox_lo", 168, [P, 4, SEQ], F32R)
    op_hi, op_lo = sb("op_hi", 176, [P, 4, SEQ], F32R), sb("op_lo", 184, [P, 4, SEQ], F32R)
    mvT = sb("mvT", 176, [P, X_HEADS, N_MEM])
    rel_row = sb("rel_row", 180, [A_HEADS, 192])
    bias_back = sb("bias_back", 184, [P, GROUPS, 4, KEYS])
    relT = sb("relT", 181, [A_HEADS, REL_BUCKETS])
    qx = sb("qx", 192, [P, X_HEADS, SEQ])
    mk = sb("mk", 200, [P, X_HEADS, N_MEM])
    mixed = [sb(f"mixed{i}", 192 + 2 * i, [P, SEQ]) for i in range(2)]
    part = sb("part", 200, [P, SEQ])
    out_at = [40, 48, 56, 64, 72, 80, 88, 196]
    wo_hi = [sb(f"wo_hi{k}", a, [P, D], F32R) for k, a in enumerate(out_at)]
    wo_lo = [sb(f"wo_lo{k}", a + 4, [P, D], F32R) for k, a in enumerate(out_at)]
    x1 = sb("x1", 128, [P, TT, D])
    g_post_b = sb("g_post_b", 144, [P, D])
    h2T_hi, h2T_lo = sb("h2T_hi", 148, [P, KT, SEQ], F32R), sb("h2T_lo", 164, [P, KT, SEQ], F32R)
    y = [sb(f"y{i}", 180 + 4 * i, [P, D]) for i in range(2)]
    g_ffn_pre_b = sb("g_ffn_pre_b", 188, [P, D])
    f_hi, f_lo = sb("f_hi", 40, [P, FT, SEQ], F32R), sb("f_lo", 84, [P, FT, SEQ], F32R)
    silu = [sb(f"silu{i}", 180 + 2 * i, [P, SEQ]) for i in range(2)]
    prod = [sb(f"prod{i}", 184 + 2 * i, [P, SEQ]) for i in range(2)]
    down_at = [188, 16, 24, 32, 196, 148, 156, 164, 172]
    ND = len(down_at)
    wd_hi = [sb(f"wd_hi{k}", a, [P, D], F32R) for k, a in enumerate(down_at)]
    wd_lo = [sb(f"wd_lo{k}", a + 4, [P, D], F32R) for k, a in enumerate(down_at)]
    w_map = sb("w_map", 204, [P, 4, P])
    square1 = sb("square1", 204, [P, D], BF16)
    ident = sb("ident", 206, [P, P])
    gain_row, ones_row = sb("gain_row", 188, [1, D]), sb("ones_row", 196, [1, P])
    small_at = [206.5]

    def small(name, shape):
        t = sb(name, small_at[0], shape)
        small_at[0] += 32 * math.ceil(4 * int(np.prod(shape[1:])) / 32) / KB
        return t

    sink = small("sink", [P, GROUPS, 4])
    scale_p = small("scale_p", [P, 4])
    inv_count = small("inv_count", [P, PAD])
    minus_half, warm = small("minus_half", [P, 1]), small("warm", [P, 1])
    part_meansq = small("part_meansq", [P, 26])
    meansq = small("meansq", [P, 20])
    rstd = small("rstd", [P, 20])
    row_max = [small(f"row_max{i}", [P, 4]) for i in range(2)]
    neg_max = [small(f"neg_max{i}", [P, 4]) for i in range(2)]
    sink_gap = [small(f"sink_gap{i}", [P, 4]) for i in range(2)]
    row_sum = [small(f"row_sum{i}", [P, 4]) for i in range(2)]
    denom = [small(f"denom{i}", [P, 4]) for i in range(2)]
    inv_denom = [small(f"inv_denom{i}", [P, 4]) for i in range(2)]
    assert small_at[0] <= 207.8

    rel_dram = nc.dram_tensor("rel_scratch", [A_HEADS, 192], F32, kind="Internal").ap()

    NORM_MEM, NORM_X, NORM_MIX, NORM_POST = 0, MT, MT + TT, MT + 3 * TT
    norm_parts = [1] * NORM_MIX + [2, 1] * TT + [2] * TT
    norm_part = [sum(norm_parts[:n]) for n in range(len(norm_parts))]

    with ExitStack() as ctx:
        pair = [ctx.enter_context(nc.psum_tensor(f"pair{i}", [P, 2, SEQ], F32)) for i in range(4)]

        def bk(i):
            return pair[i // 2][:, i % 2, :]

        def row_bank(t, h):
            return bk(2 * PAIR_OF[t] + h)

        scores = pair[2]

        def sem(name):
            return ctx.enter_context(nc.semaphore(name))

        raw_in = [sem(f"raw_in{i}") for i in range(2)]
        mem_loaded = [sem(f"mem_loaded{i}") for i in range(MT)]
        x_loaded = [sem(f"x_loaded{i}") for i in range(TT)]
        x_again = [sem(f"x_again{i}") for i in range(TT)]
        gain_loaded = {n: sem(f"gain_{n}") for n in ("mem", "pre", "post", "ffn_pre", "ffn_post")}
        rel_loaded, rel_built, rel_saved, bias_loaded = (sem(n) for n in ("rel_loaded", "rel_built", "rel_saved", "bias_loaded"))
        smalls_loaded = sem("smalls_loaded")
        consts_ready, pads_ready, warmed = sem("consts_ready"), sem("pads_ready"), sem("warmed")
        ones_ready, gain_spread, gain_copied = sem("ones_ready"), sem("gain_spread"), sem("gain_copied")
        pool_chain, vec_chain = sem("pool_chain"), sem("vec_chain")
        weights_hi, weights_split, half_split = sem("weights_hi"), sem("weights_split"), sem("half_split")
        squares_summed, rstd_ready = sem("squares_summed"), sem("rstd_ready")
        rows_normed, rows_turned, turned_hi, turned_split = (sem(n) for n in ("rows_normed", "rows_turned", "turned_hi", "turned_split"))
        tile_full, tile_copied, tile_merged = sem("tile_full"), sem("tile_copied"), sem("tile_merged")
        scores_full, scores_read, neg_max_ready, exps_done = (sem(n) for n in ("scores_full", "scores_read", "neg_max_ready", "exps_done"))
        probs_ready, probs_turned, probsT_ready = (sem(n) for n in ("probs_ready", "probs_turned", "probsT_ready"))
        o_full, o_hi_done, o_split = sem("o_full"), sem("o_hi_done"), sem("o_split")
        pool_diff_ready, map_hi_done = sem("pool_diff_ready"), sem("map_hi_done")
        sigmoid_ready, mixed_ready, mrg_hi_done, mrg_split = (sem(n) for n in ("sigmoid_ready", "mixed_ready", "mrg_hi_done", "mrg_split"))
        out_full, rows_gained, x1_ready = sem("out_full"), sem("rows_gained"), sem("x1_ready")
        ffn_full, silu_ready, prod_ready, f_hi_done, f_split = (sem(n) for n in ("ffn_full", "silu_ready", "prod_ready", "f_hi_done", "f_split"))
        down_used, down_full, result_ready, stored = (sem(n) for n in ("down_used", "down_full", "result_ready", "stored"))

        w_in_v = w_in.rearrange("(k p) n -> p k n", p=P)
        w_mem_v = w_mem_kv.rearrange("(k p) n -> p k n", p=P)
        gate_v, up_v = (w.rearrange("(k p) n -> p k n", p=P) for w in (w_gate, w_up))
        wa_v = w_branch_a.rearrange("(k p) n -> p k n", p=P)
        wp_v, wx_v = (w.rearrange("(k p) n -> p k n", p=P) for w in (w_branch_p, w_branch_x))

        def chunk_halves(first):
            kind, n = first
            if kind in ("out", "down"):
                w = w_out if kind == "out" else w_down
                return [w[P * (n + i):P * (n + i + 1), :] for i in range(2)]
            if kind == "ffn":
                v, col = (gate_v, up_v)[(n // 2) % 2], 2 * P * (n // 4)
            else:
                t, i = steps[n][0]
                if t == "p":
                    return [v[:, :, P * i:P * i + 2 * P] for v in (wp_v, wx_v)]
                if t == "mem":
                    v, col = w_mem_v, P * i
                elif t == "a":
                    v, col = wa_v, P * i
                elif t == "gate":
                    v, col = w_in_v, GATE_COL + D * (i % 6 // 2) + 2 * P * (i // 6)
                else:
                    v, col = w_in_v, {"k": K_COL, "q": 0, "qx": QX_COL, "pin": PIN_COL}[t] + P * i
            return [v[:, 4 * h:4 * h + 4, col:col + 2 * P] for h in range(2)]

        def raw_view(s):
            r = raw[s // 2 % 2]
            if stream[s][0] in ("out", "down"):
                return r[:, s % 2, :]
            return r[:, :, :].rearrange("p a (k c) -> p (a k) c", c=2 * P)[:, :, P * (s % 2):P * (s % 2) + P]

        def split_at(s):
            kind, n = stream[s]
            if kind == "step":
                return w_hi[n % 3][:, :, :], w_lo[n % 3][:, :, :]
            if kind == "ffn":
                return w_hi[n % 4][:, :, :], w_lo[n % 4][:, :, :]
            if kind == "out":
                return wo_hi[n][:, :], wo_lo[n][:, :]
            return wd_hi[n % ND][:, :], wd_lo[n % ND][:, :]

        def wait_split_free(eng, s):
            kind, n = stream[s]
            if kind == "step" and n >= 3:
                eng.wait_ge(tile_full, step_end[n - 3])
            elif kind == "out" and n < 4:
                eng.wait_ge(tile_full, tile_no[("gate", 23)] + 1)
            elif kind == "out":
                eng.wait_ge(tile_full, len(tiles))
                eng.wait_ge(mrg_split, KT)
            elif kind == "ffn" and n < 3:
                eng.wait_ge(tile_full, len(tiles))
            elif kind == "ffn" and n == 3:
                eng.wait_ge(out_full, TT)
            elif kind == "down" and n == 0:
                eng.wait_ge(rows_turned, E_V + 2 * TT)
            elif kind == "down" and n < 4:
                eng.wait_ge(ffn_full, 2 * FT - 4 + n)
            elif kind == "down" and n < ND:
                eng.wait_ge(ffn_full, 2 * FT)
            elif kind == "down":
                eng.wait_ge(down_used, n - ND + 1)

        def split_hi(eng, s):
            if s % 2 == 0:
                eng.wait_ge(raw_in[s // 2 % 2], 32 * (s // 4 + 1))
            wait_split_free(eng, s)
            eng.activation(split_at(s)[0], raw_view(s), ACT.Copy).then_inc(weights_hi, 1)

        def split_lo(eng, s):
            eng.wait_ge(weights_hi, s + 1)
            hi, lo = split_at(s)
            eng.tensor_tensor(lo, raw_view(s), hi.bitcast(F32), ALU.subtract).then_inc(weights_split, 1)

        def stream_upto(step):
            return at_stream[("step", min(step + 2, NS - 1))] + 1

        def unit_of(u):
            if u < A_UNITS:
                return "a", u // NC_, u % NC_
            return "x", (u - A_UNITS) // 2, (u - A_UNITS) % 2

        def o_at(u, hi):
            kind, a, b = unit_of(u)
            if kind == "a":
                return (oa_hi if hi else oa_lo)[:, 4 * a:4 * a + 4, CHUNK * b:CHUNK * b + CHUNK]
            return (ox_hi if hi else ox_lo)[:, a, 2 * P * b:2 * P * b + 2 * P]

        def o_psum(u):
            v = bk(7)[:, 0:2 * P]
            return v.rearrange("p (j q) -> p j q", j=4) if u < A_UNITS else v

        def turned_at(e, hi):
            t, h = (e // 2, e % 2) if e < 2 * MT else (e // 2 - MT, e % 2)
            dst = ((memT_hi, memT_lo) if e < 2 * MT else (hT_hi, hT_lo))[0 if hi else 1]
            return dst[:, 4 * h:4 * h + 4, P * t:P * t + P]

        def as4(v):
            return v.rearrange("p (j q) -> p j q", j=4)

        E_MEM, E_X = 2 * MT, 2 * MT + 2 * TT
        E_MV, E_V = E_X + 2, E_X + 4
        FFN0 = at_stream[("ffn", 0)]
        RAW_FFN = [32 * ((FFN0 + 4 + 2 * h) // 4 + 1) for h in range(2)]

        def ffn_raw(i):
            return raw_view(FFN0 + i)

        def f_tile(t, n):
            return t[:, bass.ds(n, 1), :].rearrange("p a b -> p (a b)")

        block = ctx.enter_context(nc.Block())

        @block.sync
        def _(sp):
            chunks = len(stream) // 2

            def load_chunk(c):
                if c >= 2:
                    sp.wait_ge(weights_split, 2 * c - 2)
                for h, src in enumerate(chunk_halves(stream[2 * c])):
                    dst = raw[c % 2][:, h, :]
                    if len(src.shape) == 3:
                        dst = dst.rearrange("p (k n) -> p k n", k=4)
                    sp.dma_start(dst, src).then_inc(raw_in[c % 2], 16)

            for m in range(MT):
                sp.dma_start(mem_in[:, m, :], mem[P * m:P * m + P, :]).then_inc(mem_loaded[m], 16)
            sp.dma_start(g_mem_b[:, :], row_bcast(g_mem)).then_inc(gain_loaded["mem"], 16)
            load_chunk(0)
            load_chunk(1)
            for t in range(TT):
                sp.dma_start(x_in[:, t, :], x[P * t:P * t + P, :]).then_inc(x_loaded[t], 16)
            for half in range(2):
                sp.dma_start(sink[64 * half:64 * half + 64, :, :], ap(sinks, 8 * half, [[0, 64], [4, 2], [1, 4]]))\
                  .then_inc(smalls_loaded, 16)
            sp.dma_start(scale_p[:, :], pool_scale).then_inc(smalls_loaded, 16)
            for c in range(2, 6):
                load_chunk(c)
            sp.dma_start(w_map[:, :, :], w_pool_map.rearrange("g c d -> c g d")).then_inc(smalls_loaded, 16)
            sp.wait_ge(rel_built, 1)
            sp.dma_start(rel_dram, rel_row[:, :]).then_inc(rel_saved, 16)
            for i in range(4 * GROUPS):
                if i % 3 == 0:
                    load_chunk(6 + i // 3)
                if i == 0:
                    sp.wait_ge(rel_saved, 16)
                g, pr = divmod(i, 4)
                for half in range(2):
                    head = 8 * g + 4 * (pr % 2) + pr // 2 + 2 * half
                    sp.dma_start(bias_back[64 * half:64 * half + 64, g, pr, :],
                                 ap(rel_dram, 192 * head, [[1, CHUNK], [1, KEYS]])).then_inc(bias_loaded, 16)
            last_out = at_stream[("out", KT - 1)] // 2
            for c in range(9, last_out + 1):
                load_chunk(c)
            sp.wait_ge(tile_full, len(tiles))
            for t in range(TT):
                sp.dma_start(x1[:, t, :], x[P * t:P * t + P, :]).then_inc(x_again[t], 16)
            sp.dma_start(g_post_b[:, :], row_bcast(g_mix_post)).then_inc(gain_loaded["post"], 16)
            sp.dma_start(g_ffn_pre_b[:, :], row_bcast(g_ffn_pre)).then_inc(gain_loaded["ffn_pre"], 16)
            for c in range(FFN0 // 2, FFN0 // 2 + 2):
                load_chunk(c)
            with sp.Fori(1, FT // 2) as f:
                for j, v in enumerate((gate_v, up_v)):
                    c = FFN0 // 2 + j
                    sp.wait_ge(weights_split, 2 * c - 2 + 4 * f)
                    for h in range(2):
                        sp.dma_start(raw[c % 2][:, h, :].rearrange("p (k n) -> p k n", k=4),
                                     v[:, 4 * h:4 * h + 4, bass.ds(2 * P * f, 2 * P)]).then_inc(raw_in[c % 2], 16)
            sp.wait_ge(x1_ready, TT)
            sp.dma_start(g_post_b[:, :], row_bcast(g_ffn_post)).then_inc(gain_loaded["ffn_post"], 16)
            for c in range(at_stream[("down", 0)] // 2, chunks):
                load_chunk(c)
            for t in range(TT):
                for h in range(2):
                    sp.wait_ge(result_ready, 2 * t + h + 1)
                    sp.dma_start(out[P * t:P * t + P, 512 * h:512 * h + 512], x1[:, t, 512 * h:512 * h + 512])\
                      .then_inc(stored, 16)
            sp.wait_ge(stored, 32 * TT)

        @block.gpsimd
        def _(pool):
            pool.memset(ident[:, :], 0.0).then_inc(pool_chain, 1)
            pool.memset(ones_row[:, :], 1.0).then_inc(ones_ready, 1)
            pool.memset(minus_half[:, :], -0.5).then_inc(consts_ready, 1)
            for i in range(PAD):
                pool.memset(inv_count[:, i:i + 1], 1.0 / (i + 1)).then_inc(consts_ready, 1)
            pool.wait_ge(pool_chain, 1)
            pool.affine_select(out=ident[:, :], in_=ident[:, :], compare_op=ALU.not_equal, fill=1.0, base=0,
                               pattern=[[-1, P]], channel_multiplier=1).then_inc(consts_ready, 1)
            pool.memset(k_dup[:, :, 0:CHUNK], 0.0).then_inc(pads_ready, 1)
            pool.memset(vT[:, 0:CHUNK], 0.0).then_inc(pads_ready, 1)
            pool.wait_ge(consts_ready, PAD + 2)
            chain = [1]

            def link(ins):
                chain[0] += 1
                ins.then_inc(pool_chain, 1)
                pool.wait_ge(pool_chain, chain[0])

            def inverse_rms(n):
                c = norm_part[n]
                pool.wait_ge(squares_summed, c + 1)
                link(pool.tensor_scalar(meansq[:, n:n + 1], part_meansq[:, c:c + 1], 1.0, EPS, ALU.mult, ALU.add))
                if norm_parts[n] == 2:
                    pool.wait_ge(squares_summed, c + 2)
                    link(pool.tensor_tensor(meansq[:, n:n + 1], meansq[:, n:n + 1], part_meansq[:, c + 1:c + 2], ALU.add))
                pool.tensor_tensor(rstd[:, n:n + 1], meansq[:, n:n + 1], minus_half[:, :], ALU.pow)\
                    .then_inc(rstd_ready, 1)

            for n in range(MT + TT):
                inverse_rms(n)

            pool.wait_ge(rows_turned, E_V)
            for i in range(4):
                pool.memset(pooled[i][:, 0:PAD], 0.0).then_inc(pads_ready, 1)
            pool.wait_ge(pads_ready, 6)
            for g, w in enumerate(POOL_WINDOWS):
                src = pooled[g % 2]
                pool.wait_ge(tile_copied, copied_no[("pin", g)])
                if g >= 1:
                    pool.wait_ge(tile_full, tile_no[("map", g - 1)] + 1)
                cur, d, n = src, 1, 0
                while d < w:
                    nxt = pooled[2 + n % 2]
                    link(pool.tensor_tensor(nxt[:, PAD:], cur[:, PAD:], cur[:, PAD - d:PAD + SEQ - d], ALU.add))
                    cur, d, n = nxt, 2 * d, n + 1
                diff = pooled[2 + n % 2]
                link(pool.tensor_scalar(diff[:, PAD:], cur[:, PAD:], 1.0 / w, 0.0, ALU.mult, ALU.add))
                link(pool.tensor_tensor(diff[:, PAD:PAD + w - 1], cur[:, PAD:PAD + w - 1], inv_count[:, 0:w - 1], ALU.mult))
                pool.tensor_tensor(diff[:, PAD:], diff[:, PAD:], src[:, PAD:], ALU.subtract).then_inc(pool_diff_ready, 1)

            for n in range(NORM_MIX, NORM_MIX + 3 * TT):
                inverse_rms(n)

        def diff_at(g):
            return pooled[2 + (g + 1) % 2]

        @block.scalar
        def _(act):
            act.dma_start(gain_row[:, :], ap(g_mix_pre, 0, [[D, 1], [1, D]])).then_inc(gain_loaded["pre"], 16)
            act.dma_start(relT[:, :], rel_bias).then_inc(rel_loaded, 16)
            act.wait_ge(consts_ready, 1)
            act.activation(warm[:, :], minus_half[:, :], ACT.Square).then_inc(warmed, 1)

            def mean_square(src, n, scratch, h=0):
                c = norm_part[n] + h
                act.activation(scratch, src, ACT.Square, scale=1.0 / math.sqrt(D),
                               accum_out=part_meansq[:, c:c + 1]).then_inc(squares_summed, 1)
                act.wait_ge(squares_summed, c + 1)

            def turn_hi(e):
                act.wait_ge(rows_turned, e + 1)
                act.activation(turned_at(e, True), as4(bk(4 + e % 4)), ACT.Copy).then_inc(turned_hi, 1)

            def probsT_copy(u):
                act.wait_ge(probs_turned, u + 1)
                if u >= 1:
                    act.wait_ge(o_full, u)
                act.activation(probsT[:, :, :], as4(bk(6)), ACT.Copy).then_inc(probsT_ready, 1)

            def exps(u):
                kind, a, b = unit_of(u)
                act.wait_ge(neg_max_ready, u + 1)
                pr = probs[u % 2]
                if kind == "a":
                    for i in range(4):
                        act.activation(pr[:, i, :], pr[:, i, :], ACT.Exp, bias=neg_max[u % 2][:, i:i + 1],
                                       accum_out=row_sum[u % 2][:, i:i + 1])
                    act.activation(sink_gap[u % 2][:, :], sink_gap[u % 2][:, :], ACT.Exp).then_inc(exps_done, 1)
                else:
                    act.wait_ge(probs_turned, u - 1)
                    flat = pr[:, :, :].rearrange("p (t m) k -> p t (m k)", t=2)
                    for i in range(2):
                        ins = act.activation(flat[:, i, :], scores[:, i, 0:N_MEM], ACT.Exp,
                                             bias=neg_max[u % 2][:, i:i + 1], scale=X_SCALE,
                                             accum_out=row_sum[u % 2][:, i:i + 1])
                    ins.then_inc(exps_done, 1)

            def o_hi(u):
                act.wait_ge(o_full, u + 1)
                act.activation(o_at(u, True), o_psum(u), ACT.Copy).then_inc(o_hi_done, 1)

            def take(t):
                kind, i = t
                n = tile_no[t]
                src = bk(n % 4)
                act.wait_ge(tile_full, n + 1)
                if kind == "mem":
                    dst = mk[:, i, :] if i < X_HEADS else mvT[:, i - X_HEADS, :]
                    act.activation(dst, src[:, 0:N_MEM], ACT.Copy).then_inc(tile_copied, 1)
                elif kind == "k":
                    act.wait_ge(pads_ready, 2)
                    for g in range(GROUPS):
                        for half in range(2):
                            ins = act.activation(k_dup[64 * half:64 * half + 64, g, CHUNK:],
                                                 src[64 * g:64 * g + 64, :], ACT.Copy)
                    ins.then_inc(tile_copied, 1)
                elif kind == "v":
                    act.activation(vT[:, CHUNK:], src, ACT.Copy).then_inc(tile_copied, 1)
                elif kind == "q":
                    act.activation(q[:, i // 2, :, i % 2, :], src.rearrange("p (c t) -> p c t", c=NC_), ACT.Copy)\
                        .then_inc(tile_copied, 1)
                elif kind == "qx":
                    act.activation(qx[:, i, :], src, ACT.Copy).then_inc(tile_copied, 1)
                elif kind == "pin":
                    if i >= 2:
                        act.wait_ge(pool_diff_ready, i - 1)
                    act.wait_ge(rows_turned, E_V)
                    act.activation(pooled[i % 2][:, PAD:], src, ACT.Copy).then_inc(tile_copied, 1)
                elif kind == "gate":
                    if i >= 12:
                        act.wait_ge(mrg_split, 2 * (i // 6) - 2)
                    act.activation(gates[:, i % 12, :], src, ACT.Copy).then_inc(tile_copied, 1)
                elif kind == "map":
                    act.activation(op_hi[:, i, :], src, ACT.Copy, scale=scale_p[:, i:i + 1]).then_inc(map_hi_done, 1)

            def sigmoids(j):
                for b in range(3):
                    i = 6 * (j // 2) + 2 * b + j % 2
                    act.wait_ge(tile_copied, copied_no[("gate", i)])
                    v = gates[:, i % 12, :]
                    act.activation(v, v, ACT.Sigmoid).then_inc(sigmoid_ready, 1)

            def merged_hi(j):
                act.wait_ge(mixed_ready, j + 1)
                act.activation(mrg_hi[:, j, :], mixed[j % 2][:, :], ACT.Copy).then_inc(mrg_hi_done, 1)

            def turned_x(t):
                for h in range(2):
                    turn_hi(E_MEM + 2 * t + h)

            for m in range(MT):
                act.wait_ge(mem_loaded[m], 16)
                mean_square(mem_in[:, m, :], NORM_MEM + m, square0[:, :])
            for m in range(MT):
                for h in range(2):
                    turn_hi(2 * m + h)
                split_hi(act, m)
            act.wait_ge(gain_spread, 2)
            act.activation(g_mix_pre_b[:, :], pair[1][:, :, :].rearrange("p a b -> p (a b)"), ACT.Copy)\
               .then_inc(gain_copied, 1)

            done = 2
            for s in range(NS):
                u = s - UNIT0
                if 0 <= u - 2 < UNITS:
                    o_hi(u - 2)
                if s >= 2 and steps[s - 2][0][0] == "p":
                    merged_hi(steps[s - 2][0][1])
                if s - 1 == X_AFTER[-1]:
                    turned_x(TT - 1)
                while done < stream_upto(s):
                    split_hi(act, done)
                    done += 1
                if 0 <= u - 1 < UNITS:
                    probsT_copy(u - 1)
                if s >= 1:
                    for t in steps[s - 1]:
                        if t in copied_no or t[0] == "map":
                            take(t)
                if s < TT:
                    act.wait_ge(x_loaded[s], 16)
                    mean_square(x_in[:, s, :], NORM_X + s, square0[:, :])
                if s - 1 in X_AFTER[:-1]:
                    turned_x(X_AFTER.index(s - 1))
                if 0 <= u < UNITS:
                    exps(u)
                if steps[s][0][0] == "a":
                    sigmoids(steps[s][0][1])
            for j in (KT - 2, KT - 1):
                merged_hi(j)

            def h2_hi(t):
                for h in range(2):
                    act.wait_ge(rows_turned, E_V + 2 * t + h + 1)
                    act.activation(h2T_hi[:, 4 * h:4 * h + 4, P * t:P * t + P], as4(row_bank(t, h)), ACT.Copy)\
                        .then_inc(turned_hi, 1)

            n_out = at_stream[("ffn", 0)]
            while done < n_out:
                split_hi(act, done)
                done += 1
            for t in range(TT):
                if t >= 1:
                    h2_hi(t - 1)
                act.wait_ge(out_full, t + 1)
                for h in range(2):
                    mean_square(row_bank(t, h), NORM_MIX + 2 * t, square1[:, 0:512], h)
                act.wait_ge(x1_ready, t + 1)
                mean_square(x1[:, t, :], NORM_MIX + 2 * t + 1, square1[:, :])
                if t < 3:
                    split_hi(act, done)
                    done += 1
            split_hi(act, done)
            done += 1
            h2_hi(TT - 1)

            def ffn_step(f, i, first=False, last=False):
                act.wait_ge(ffn_full, 4 * f + i + 1)
                if last:
                    split_hi(act, at_stream[("down", i)])
                else:
                    if i % 2 == 0:
                        act.wait_ge(raw_in[(FFN0 + i) // 2 % 2], RAW_FFN[i // 2] + 32 * f)
                    act.activation(w_hi[i][:, :, :], ffn_raw(i), ACT.Copy).then_inc(weights_hi, 1)
                if i < 2:
                    if not first:
                        act.wait_ge(prod_ready, 2 * f - 1 + i)
                    act.activation(silu[i][:, :], bk(i), ACT.Silu).then_inc(silu_ready, 1)
                else:
                    act.wait_ge(prod_ready, 2 * f + i - 1)
                    act.activation(f_tile(f_hi, 2 * f + i - 2), prod[i - 2][:, :], ACT.Copy).then_inc(f_hi_done, 1)

            for i in range(4):
                ffn_step(0, i, first=True)
            with act.Fori(1, FT // 2 - 1) as f:
                for i in range(4):
                    ffn_step(f, i)
            for i in range(4):
                ffn_step(FT // 2 - 1, i, last=True)
            done = at_stream[("down", 4)]
            while done < len(stream):
                split_hi(act, done)
                done += 1
            for t in range(TT):
                for h in range(2):
                    act.wait_ge(down_full, 2 * t + h + 1)
                    mean_square(row_bank(t, h), NORM_POST + t, square1[:, 0:512], h)

        @block.vector
        def _(dve):
            chain = [0]

            def link(ins):
                chain[0] += 1
                ins.then_inc(vec_chain, 1)
                dve.wait_ge(vec_chain, chain[0])

            def norm_rows(dst, src, n, gain):
                dve.wait_ge(rstd_ready, n + 1)
                dve.scalar_tensor_tensor(out=dst, in0=src, scalar=rstd[:, n:n + 1], in1=gain, op0=ALU.mult,
                                         op1=ALU.mult).then_inc(rows_normed, 1)

            def turn_lo(e):
                dve.wait_ge(turned_hi, e + 1)
                dve.tensor_tensor(turned_at(e, False), as4(bk(4 + e % 4)), turned_at(e, True).bitcast(F32),
                                  ALU.subtract).then_inc(turned_split, 1)

            def turned_x(t):
                for h in range(2):
                    turn_lo(E_MEM + 2 * t + h)

            def maxima(u):
                kind, a, b = unit_of(u)
                pr, mx = probs[u % 2], row_max[u % 2]
                dve.wait_ge(scores_full, u + 1)
                if kind == "a":
                    if u == 0:
                        dve.wait_ge(bias_loaded, 16 * 16)
                        v = bias_back[:, :, :, :]
                        back = bass.AP(v.tensor, v.offset + KEYS - 1, [list(v.ap[0]), [KEYS, 4 * GROUPS], [-1, KEYS]])
                        link(dve.tensor_copy(bias[:, :, :, :].rearrange("p g a k -> p (g a) k"), back))
                        dve.wait_ge(smalls_loaded, 16 * 4)
                    if u >= 2:
                        dve.wait_ge(probs_turned, u - 1)
                    dve.scalar_tensor_tensor(out=pr[:, :, :].rearrange("p (a b) k -> p a b k", a=2),
                                             in0=scores[:, :, 0:2 * KEYS].rearrange("p a (b k) -> p a b k", b=2),
                                             scalar=A_SCALE,
                                             in1=bias[:, a, :, :].rearrange("p (a b) k -> p a b k", a=2),
                                             op0=ALU.mult, op1=ALU.add).then_inc(scores_read, 1)
                    dve.wait_ge(scores_read, u + 1)
                    if b == 0:
                        link(dve.memset(pr[:, :, 0:CHUNK], -1e30))
                    link(dve.tensor_reduce(mx[:, :], pr[:, :, :], AX_X, ALU.max))
                    link(dve.tensor_tensor(mx[:, :], mx[:, :], sink[:, a, :], ALU.max))
                    dve.tensor_tensor(sink_gap[u % 2][:, :], sink[:, a, :], mx[:, :], ALU.subtract)
                    dve.tensor_scalar(neg_max[u % 2][:, :], mx[:, :], -1.0, None, ALU.mult).then_inc(neg_max_ready, 1)
                else:
                    link(dve.tensor_reduce(mx[:, 0:2], scores[:, :, 0:N_MEM], AX_X, ALU.max))
                    dve.tensor_scalar(neg_max[u % 2][:, 0:2], mx[:, 0:2], -X_SCALE, None, ALU.mult)\
                       .then_inc(neg_max_ready, 1)

            def normalise(u):
                kind, a, b = unit_of(u)
                pr, r = probs[u % 2], inv_denom[u % 2]
                dve.wait_ge(exps_done, u + 1)
                if kind == "a":
                    link(dve.tensor_tensor(denom[u % 2][:, :], row_sum[u % 2][:, :], sink_gap[u % 2][:, :], ALU.add))
                    link(dve.reciprocal(r[:, :], denom[u % 2][:, :]))
                    v, n, w = pr[:, :, :], 4, KEYS
                else:
                    link(dve.reciprocal(r[:, 0:2], row_sum[u % 2][:, 0:2]))
                    v, n, w = pr[:, :, :].rearrange("p (t m) k -> p t (m k)", t=2), 2, N_MEM
                dve.tensor_tensor(v, v, r[:, 0:n].unsqueeze(2).to_broadcast([P, n, w]), ALU.mult)\
                   .then_inc(probs_ready, 1)

            def o_lo(u):
                dve.wait_ge(o_hi_done, u + 1)
                dve.tensor_tensor(o_at(u, False), o_psum(u), o_at(u, True).bitcast(F32), ALU.subtract)\
                   .then_inc(o_split, 1)

            def map_lo(g):
                dve.wait_ge(map_hi_done, g + 1)
                dve.scalar_tensor_tensor(out=op_lo[:, g, :], in0=bk(tile_no[("map", g)] % 4), scalar=scale_p[:, g:g + 1],
                                         in1=op_hi[:, g, :].bitcast(F32), op0=ALU.mult, op1=ALU.subtract)\
                   .then_inc(tile_merged, 1)

            def merge(t):
                kind, j = t
                n = tile_no[t]
                b = "axp".index(kind)
                gate = gates[:, (6 * (j // 2) + 2 * b + j % 2) % 12, :]
                dve.wait_ge(tile_full, n + 1)
                dve.wait_ge(sigmoid_ready, 3 * j + 3)
                if kind == "p" and j >= 1:
                    dve.wait_ge(mixed_ready, j)
                dst = mixed[j % 2] if kind == "a" else part
                dve.tensor_tensor(dst[:, :], bk(n % 4), gate, ALU.mult).then_inc(tile_merged, 1)
                dve.wait_ge(tile_merged, merged_no[t])
                if kind != "a":
                    ins = dve.tensor_tensor(mixed[j % 2][:, :], mixed[j % 2][:, :], part[:, :], ALU.add)
                    if kind == "p":
                        link(ins)
                    else:
                        ins.then_inc(mixed_ready, 1)

            def merged_lo(j):
                dve.wait_ge(mrg_hi_done, j + 1)
                dve.tensor_tensor(mrg_lo[:, j, :], mixed[j % 2][:, :], mrg_hi[:, j, :].bitcast(F32), ALU.subtract)\
                   .then_inc(mrg_split, 1)
                dve.wait_ge(mrg_split, j + 1)

            dve.wait_ge(gain_loaded["mem"], 16)
            for m in range(MT):
                norm_rows(mem_in[:, m, :], mem_in[:, m, :], NORM_MEM + m, g_mem_b[:, :])
            turn_lo(0)
            turn_lo(1)
            dve.wait_ge(weights_hi, 1)
            hi, lo = split_at(0)
            for h, signal in enumerate((half_split, weights_split)):
                if h == 1:
                    turn_lo(2)
                ks = slice(4 * h, 4 * h + 4)
                dve.tensor_tensor(lo[:, ks, :], raw_view(0)[:, ks, :], hi[:, ks, :].bitcast(F32), ALU.subtract)\
                   .then_inc(signal, 1)
            turn_lo(3)
            split_lo(dve, 1)
            dve.wait_ge(gain_copied, 1)

            done = 2
            for s in range(NS):
                u = s - UNIT0
                if 0 <= u - 2 < UNITS:
                    o_lo(u - 2)
                if s >= 2 and steps[s - 2][0][0] == "p":
                    merged_lo(steps[s - 2][0][1])
                if 0 <= u < UNITS:
                    maxima(u)
                if s - 1 == X_AFTER[-1]:
                    turned_x(TT - 1)
                while done < stream_upto(s):
                    split_lo(dve, done)
                    done += 1
                if s < TT:
                    norm_rows(x_in[:, s, :], x_in[:, s, :], NORM_X + s, g_mix_pre_b[:, :])
                if s >= 1:
                    for t in steps[s - 1]:
                        if t[0] == "map":
                            map_lo(t[1])
                        elif t[0] in "axp":
                            merge(t)
                if s - 1 in X_AFTER[:-1]:
                    turned_x(X_AFTER.index(s - 1))
                if s == X_AFTER[-1] + 1:
                    dve.wait_ge(rel_loaded, 16)
                    ranges = bucket_ranges()
                    for n, (a, b, bucket) in enumerate(ranges):
                        ins = dve.tensor_copy(rel_row[:, a:b], relT[:, bucket:bucket + 1].to_broadcast([A_HEADS, b - a]))
                        if n == len(ranges) - 1:
                            ins = dve.memset(rel_row[:, b:192], 0.0)
                    ins.then_inc(rel_built, 1)
                if s == 11:
                    for e in range(E_X, E_V):
                        dve.wait_ge(rows_turned, e + 1)
                        if e < E_MV:
                            dst = mv[:, e - E_X, :, :]
                        else:
                            dst = v_c[:, 4 * (e - E_MV):4 * (e - E_MV) + 4, :]
                        dve.tensor_copy(dst, as4(bk(4 + e % 4))).then_inc(turned_split, 1)
                if 0 <= u < UNITS:
                    normalise(u)
            for t in steps[NS - 1]:
                merge(t)
            for j in (KT - 2, KT - 1):
                merged_lo(j)

            def gained(t, h, n, number):
                dve.wait_ge(squares_summed, norm_part[n] + h + 1)
                dve.tensor_tensor(y[t % 2][:, 512 * h:512 * h + 512], row_bank(t, h),
                                  g_post_b[:, 512 * h:512 * h + 512], ALU.mult).then_inc(rows_gained, 1)
                dve.wait_ge(rows_gained, number)

            def add_rows(t, n, lo, hi):
                return dve.scalar_tensor_tensor(out=x1[:, t, lo:hi], in0=y[t % 2][:, lo:hi], scalar=rstd[:, n:n + 1],
                                                in1=x1[:, t, lo:hi], op0=ALU.mult, op1=ALU.add)

            def h2_lo(t):
                for h in range(2):
                    dve.wait_ge(turned_hi, E_X + 2 * t + h + 1)
                    dst = (slice(None), slice(4 * h, 4 * h + 4), slice(P * t, P * t + P))
                    dve.tensor_tensor(h2T_lo[dst], as4(row_bank(t, h)), h2T_hi[dst].bitcast(F32), ALU.subtract)\
                       .then_inc(turned_split, 1)

            while done < at_stream[("ffn", 0)]:
                split_lo(dve, done)
                done += 1
            dve.wait_ge(gain_loaded["post"], 16)
            dve.wait_ge(gain_loaded["ffn_pre"], 16)
            for t in range(TT):
                if t >= 1:
                    h2_lo(t - 1)
                dve.wait_ge(x_again[t], 16)
                if t >= 2:
                    dve.wait_ge(rows_turned, E_V + 2 * t - 2)
                for h in range(2):
                    gained(t, h, NORM_MIX + 2 * t, 2 * t + h + 1)
                dve.wait_ge(rstd_ready, NORM_MIX + 2 * t + 1)
                add_rows(t, NORM_MIX + 2 * t, 0, D).then_inc(x1_ready, 1)
                if t < 3:
                    split_lo(dve, done)
                    done += 1
                norm_rows(y[t % 2][:, :], x1[:, t, :], NORM_MIX + 2 * t + 1, g_ffn_pre_b[:, :])
            split_lo(dve, done)
            done += 1
            h2_lo(TT - 1)

            def ffn_step(f, i, last=False):
                dve.wait_ge(ffn_full, 4 * f + i + 1)
                if i >= 2:
                    dve.wait_ge(silu_ready, 2 * f + i - 1)
                    dve.tensor_tensor(prod[i - 2][:, :], silu[i - 2][:, :], bk(i), ALU.mult).then_inc(prod_ready, 1)
                if last:
                    split_lo(dve, at_stream[("down", i)])
                else:
                    dve.wait_ge(weights_hi, FFN0 + 4 + i + 1 + 4 * f)
                    dve.tensor_tensor(w_lo[i][:, :, :], ffn_raw(i), w_hi[i][:, :, :].bitcast(F32), ALU.subtract)\
                       .then_inc(weights_split, 1)
                if i >= 2:
                    dve.wait_ge(f_hi_done, 2 * f + i - 1)
                    n = 2 * f + i - 2
                    dve.tensor_tensor(f_tile(f_lo, n), prod[i - 2][:, :], f_tile(f_hi, n).bitcast(F32), ALU.subtract)\
                       .then_inc(f_split, 1)
                    dve.wait_ge(f_split, 2 * f + i - 1)

            for i in range(4):
                ffn_step(0, i)
            with dve.Fori(1, FT // 2 - 1) as f:
                for i in range(4):
                    ffn_step(f, i)
            for i in range(4):
                ffn_step(FT // 2 - 1, i, last=True)
            done = at_stream[("down", 4)]
            while done < len(stream):
                split_lo(dve, done)
                done += 1
            dve.wait_ge(gain_loaded["ffn_post"], 16)
            for t in range(TT):
                if t >= 2:
                    dve.wait_ge(result_ready, 2 * t - 2)
                for h in range(2):
                    gained(t, h, NORM_POST + t, 2 * TT + 2 * t + h + 1)
                dve.wait_ge(rstd_ready, NORM_POST + t + 1)
                for h in range(2):
                    add_rows(t, NORM_POST + t, 512 * h, 512 * h + 512).then_inc(result_ready, 1)

        @block.tensor
        def _(pe):
            def three(dst, whi, wlo, xhi, xlo, first, last, swap=False):
                pairs = [(whi, xhi), (whi, xlo), (wlo, xhi)]
                if swap:
                    pairs = [(xhi, whi), (xhi, wlo), (xlo, whi)]
                for n, (a, b) in enumerate(pairs):
                    ins = pe.matmul(dst, a, b, start=first and n == 0, stop=last and n == 2)
                return ins

            def turn_to(dst, src):
                for i in range(4):
                    ins = pe.transpose(dst[:, P * i:P * i + P], src[:, P * i:P * i + P], ident[:, :])
                ins.then_inc(rows_turned, 1)

            def turn_rows(src, e):
                pe.wait_ge(rows_normed, e // 2 + 1)
                if E_MEM <= e:
                    pe.wait_ge(turned_split, e - 3)
                turn_to(bk(4 + e % 4), src)

            def tile(t, s, midway=None):
                kind, i = t
                n = tile_no[t]
                dst = bk(n % 4)
                if n >= 4:
                    before = tiles[n - 4]
                    if before in copied_no:
                        pe.wait_ge(tile_copied, copied_no[before])
                    else:
                        pe.wait_ge(tile_merged, merged_no[before])
                if kind == "map":
                    pe.wait_ge(pool_diff_ready, i + 1)
                    pe.matmul(dst, w_map[:, i, :], diff_at(i)[:, PAD:], start=True, stop=True).then_inc(tile_full, 1)
                    return
                whi, wlo = w_hi[s % 3], w_lo[s % 3]
                if s == 2:
                    pe.wait_ge(gain_copied, 1)
                if s == 0:
                    pe.wait_ge(half_split, 1)
                else:
                    pe.wait_ge(weights_split, at_stream[("step", s)] + 1)
                if kind == "mem":
                    xhi, xlo, dst = memT_hi, memT_lo, dst[:, 0:N_MEM]
                elif kind in ("a", "p", "x"):
                    xhi, xlo = {"a": (oa_hi, oa_lo), "p": (op_hi, op_lo), "x": (ox_hi, ox_lo)}[kind]
                else:
                    xhi, xlo = hT_hi, hT_lo
                if s == 0:
                    pe.wait_ge(turned_split, E_MEM - 1)
                if kind == "k":
                    pe.wait_ge(turned_split, E_X)
                if kind == "a":
                    pe.wait_ge(o_split, A_UNITS)
                if kind == "p":
                    pe.wait_ge(tile_merged, merged_no[("map", 3)])
                if kind == "x":
                    pe.wait_ge(o_split, UNITS)
                ks = {"p": range(4), "x": range(4, 8)}.get(kind, range(8))
                for k in ks:
                    kx = k - 4 if kind == "x" else k
                    if s == 0 and k == 4:
                        pe.wait_ge(weights_split, 1)
                        pe.wait_ge(turned_split, E_MEM)
                    ins = three(dst, whi[:, k, :], wlo[:, k, :], xhi[:, kx, :], xlo[:, kx, :],
                                k == ks[0], k == ks[-1])
                    if midway and k == ks[len(ks) // 2 - 1]:
                        midway()
                ins.then_inc(tile_full, 1)

            def unit_scores(u):
                kind, a, b = unit_of(u)
                if u >= 1:
                    pe.wait_ge(scores_read if u <= A_UNITS else exps_done, u)
                else:
                    pe.wait_ge(turned_split, E_V)
                if kind == "a":
                    pe.wait_ge(tile_copied, copied_no[("q", 4 * a + 3)])
                    for pr in range(4):
                        lo = 64 * (pr // 2)
                        ins = pe.matmul(scores[:, pr // 2, KEYS * (pr % 2):KEYS * (pr % 2) + KEYS],
                                        q[lo:lo + 64, 2 * a + pr % 2, b, :, :].rearrange("p j t -> p (j t)"),
                                        k_dup[lo:lo + 64, a, CHUNK * b:CHUNK * b + KEYS], start=True, stop=True)
                else:
                    pe.wait_ge(tile_copied, copied_no[("qx", a)])
                    for i in range(2):
                        at = P * (2 * b + i)
                        ins = pe.matmul(scores[:, i, 0:N_MEM], qx[:, a, at:at + P], mk[:, a, :], start=True, stop=True)
                ins.then_inc(scores_full, 1)

            def unit_turn(u):
                pe.wait_ge(probs_ready, u + 1)
                if u >= 1:
                    pe.wait_ge(probsT_ready, u)
                for i in range(4):
                    dst = i if u < A_UNITS else 2 * (i % 2) + i // 2
                    ins = pe.transpose(bk(6)[:, P * dst:P * dst + P], probs[u % 2][:, i, :], ident[:, :])
                ins.then_inc(probs_turned, 1)

            def unit_out(u):
                kind, a, b = unit_of(u)
                pe.wait_ge(probsT_ready, u + 1)
                if u >= 1:
                    pe.wait_ge(o_split, u)
                if kind == "a":
                    for half in range(2):
                        ins = pe.matmul(bk(7)[64 * half:64 * half + 64, 0:2 * P], v_c[:, b, 64 * a:64 * a + 64],
                                        probsT[:, 2 * half:2 * half + 2, :], start=True, stop=True)
                else:
                    for m in range(MT):
                        ins = pe.matmul(bk(7)[:, 0:2 * P], mv[:, m, a, :], probsT[:, 2 * m:2 * m + 2, :],
                                        start=(m == 0), stop=(m == MT - 1))
                ins.then_inc(o_full, 1)

            def warm_up(n, bank):
                for _ in range(n):
                    pe.transpose(bk(bank)[:, 0:P], ident[:, :], ident[:, :])

            pe.wait_ge(consts_ready, PAD + 2)
            for m in range(MT):
                warm_up(WARM_UP[m], 7)
                for h in range(2):
                    turn_rows(mem_in[:, m, 512 * h:512 * h + 512], 2 * m + h)
            pe.wait_ge(ones_ready, 1)
            pe.wait_ge(gain_loaded["pre"], 16)
            for h in range(2):
                pe.matmul(bk(2 + h), ones_row[:, :], gain_row[:, 512 * h:512 * h + 512], start=True, stop=True)\
                  .then_inc(gain_spread, 1)
                warm_up(WARM_UP[MT], 1)
            for s in range(NS):
                u = s - UNIT0
                if 0 <= u < UNITS:
                    unit_scores(u)
                midway = (lambda: unit_turn(u - 1)) if 0 <= u - 1 < UNITS else None
                for t in steps[s]:
                    tile(t, s, midway)
                    midway = None
                if 0 <= u - 1 < UNITS:
                    unit_out(u - 1)
                if s in X_AFTER:
                    t = X_AFTER.index(s)
                    for h in range(2):
                        turn_rows(x_in[:, t, 512 * h:512 * h + 512], E_MEM + 2 * t + h)
                if s == 10:
                    pe.wait_ge(tile_copied, copied_no[("v", 0)])
                    for m in range(MT):
                        e = E_X + m
                        pe.wait_ge(turned_split, e - 3)
                        for h in range(X_HEADS):
                            ins = pe.transpose(bk(4 + e % 4)[:, P * h:P * h + P], mvT[:, h, P * m:P * m + P], ident[:, :])
                        ins.then_inc(rows_turned, 1)
                    for half in range(2):
                        e = E_MV + half
                        pe.wait_ge(turned_split, e - 3)
                        for i in range(4):
                            c = 4 * half + i
                            ins = pe.transpose(bk(4 + e % 4)[:, P * i:P * i + P], vT[:, CHUNK * c:CHUNK * c + P], ident[:, :])
                        ins.then_inc(rows_turned, 1)

            def turn_h2(t):
                pe.wait_ge(rows_normed, MT + TT + t + 1)
                for h in range(2):
                    turn_to(row_bank(t, h), y[t % 2][:, 512 * h:512 * h + 512])

            for t in range(TT):
                if t == 1:
                    pe.wait_ge(tile_merged, merged_no[tiles[-1]])
                for k in range(KT):
                    if t == 0:
                        pe.wait_ge(weights_split, at_stream[("out", k)] + 1)
                        pe.wait_ge(mrg_split, k + 1)
                    for h in range(2):
                        ins = three(row_bank(t, h), wo_hi[k][:, 512 * h:512 * h + 512], wo_lo[k][:, 512 * h:512 * h + 512],
                                    mrg_hi[:, k, P * t:P * t + P], mrg_lo[:, k, P * t:P * t + P],
                                    k == 0, k == KT - 1, swap=True)
                    if t >= 1 and k == 6:
                        turn_h2(t - 1)
                ins.then_inc(out_full, 1)

            def ffn_part(e, lo, hi):
                for k in range(KT):
                    ins = three(bk(e % 4)[:, lo:hi], w_hi[e % 4][:, k, :], w_lo[e % 4][:, k, :],
                                h2T_hi[:, k, lo:hi], h2T_lo[:, k, lo:hi], k == 0, k == KT - 1)
                return ins

            for i in range(4):
                if i == 3:
                    turn_h2(TT - 1)
                pe.wait_ge(weights_split, FFN0 + i + 1)
                pe.wait_ge(turned_split, E_V + (4 if i < 2 else 6))
                ffn_part(i, 0, SEQ // 2)
            pe.wait_ge(turned_split, E_V + 8)
            for i in range(4):
                ffn_part(i, SEQ // 2, SEQ).then_inc(ffn_full, 1)

            with pe.Fori(1, FT // 2) as f:
                for i in range(4):
                    pe.wait_ge(weights_split, FFN0 + i + 1 + 4 * f)
                    pe.wait_ge(silu_ready if i < 2 else prod_ready, 2 * f - 1 + i % 2)
                    ffn_part(i, 0, SEQ).then_inc(ffn_full, 1)

            def down(t, k, halves=(0, 1)):
                s = k % ND
                for h in halves:
                    ins = three(row_bank(t, h), wd_hi[s][:, 512 * h:512 * h + 512], wd_lo[s][:, 512 * h:512 * h + 512],
                                f_hi[:, k, P * t:P * t + P], f_lo[:, k, P * t:P * t + P],
                                k == 0, k == FT - 1, swap=True)
                return ins

            pe.wait_ge(turned_split, E_V + 8)
            for k in range(FT - TAIL):
                pe.wait_ge(weights_split, at_stream[("down", k)] + 1)
                pe.wait_ge(f_split, k + 1)
                for t in (0, 3, 1, 2):
                    if k == 0 and t == 1:
                        pe.wait_ge(silu_ready, FT)
                        pe.wait_ge(prod_ready, FT)
                    ins = down(t, k)
                ins.then_inc(down_used, 1)
            for t in range(TT):
                for h in range(2):
                    for k in range(FT - TAIL, FT):
                        if t == 0 and h == 0:
                            pe.wait_ge(weights_split, at_stream[("down", k)] + 1)
                            pe.wait_ge(f_split, k + 1)
                        ins = down(t, k, (h,))
                    ins.then_inc(down_full, 1)


_INS = ["x", "mem", "norm_mix_pre", "norm_mix_post", "norm_mem", "w_in", "rel_bias", "attn_sinks", "w_mem_kv",
        "w_pool_map", "pool_scale", "w_branch_a", "w_branch_x", "w_branch_p", "w_out", "norm_ffn_pre",
        "norm_ffn_post", "w_ffn_gate", "w_ffn_up", "w_ffn_down"]


def kernel(**inputs):
    import concourse.bacc as bacc
    from concourse.bass_utils import run_bass_kernel_spmd

    nc = bacc.Bacc("TRN2", target_bir_lowering=False, num_devices=1)
    arrays, args = {}, []
    for name in _INS:
        a = np.ascontiguousarray(inputs[name])
        if name != "rel_bias":
            a = a[0]
        if name == "rel_bias":
            a = a.T
        elif name == "pool_scale":
            a = a.reshape(4, P).T
        elif name == "attn_sinks":
            a = a.reshape(GROUPS, 2, 2, 2).transpose(2, 0, 3, 1)
        a = np.ascontiguousarray(a)
        arrays[f"in_{name}"] = a
        args.append(nc.dram_tensor(f"in_{name}", a.shape, mybir.dt.from_np(a.dtype), kind="ExternalInput").ap())
    result = nc.dram_tensor("result", (SEQ, D), F32, kind="ExternalOutput").ap()
    encoder_block(nc, *args, result)
    r = run_bass_kernel_spmd(nc, [arrays], core_ids=[0])
    return r.results[0]["result"].reshape(1, SEQ, D)
```
